# Optimizing a Trainium2 kernel written in Bass

```python
import jax, jax.numpy as jnp
from jax import lax
import numpy as np
import math

D_MODEL = 1024
BATCH = 1
SEQ = 256
DEPTH = 2

BLOCK = 128
HEAD_DIM = 64
N_HEADS_FOX = 16
N_HEADS_DIL = 16
WIDTH_FOX = N_HEADS_FOX * HEAD_DIM
WIDTH_DIL = N_HEADS_DIL * HEAD_DIM
DIL_PATTERNS = ((128, 1), (512, 4), (2048, 16))
N_HEADS_RET = 4
RET_QK_DIM = 256
RET_V_DIM = 512
RET_CHUNK = 128
ROT_BASE = 10000.0
EPS = 1e-6
NEG = -1e30
N_EVEN = (DEPTH + 1) // 2
N_ODD = DEPTH // 2
EVEN_IN = 4 * WIDTH_FOX + N_HEADS_FOX + 4 * WIDTH_DIL
EVEN_MIX = WIDTH_FOX + WIDTH_DIL
ODD_IN = 2 * N_HEADS_RET * RET_QK_DIM + 2 * N_HEADS_RET * RET_V_DIM
ODD_MIX = N_HEADS_RET * RET_V_DIM


f32 = jnp.float32

def rms_norm(x, g):
    xf = x.astype(f32)
    y = xf * lax.rsqrt(jnp.mean(xf * xf, axis=-1, keepdims=True) + EPS)
    return (y * g.astype(f32)).astype(x.dtype)

def forgetting_attention(q, k, v, log_f):
    Bsz, S, H, hd = q.shape
    scale = hd ** -0.5
    c = jnp.cumsum(log_f, axis=1).transpose(0, 2, 1)
    outs = []
    for i in range(S // BLOCK):
        q0, e = i * BLOCK, (i + 1) * BLOCK
        s = jnp.einsum('bqhd,bkhd->bhqk', q[:, q0:e], k[:, :e]).astype(f32) * scale
        s = s + c[:, :, q0:e, None] - c[:, :, None, :e]
        causal = jnp.arange(e)[None, :] <= (q0 + jnp.arange(BLOCK))[:, None]
        p = jax.nn.softmax(jnp.where(causal, s, NEG), axis=-1)
        outs.append(jnp.einsum('bhqk,bkhd->bqhd', p.astype(v.dtype), v[:, :e]))
    return jnp.concatenate(outs, axis=1)

def dilated_pattern(q, k, v, window, dilation):
    Bsz, S, H, hd = q.shape
    n_keys = window // dilation
    span = dilation * BLOCK
    Sp = -(-S // span) * span
    L = Sp // dilation
    nb = L // BLOCK

    def streams(t):
        t = jnp.pad(t, ((0, 0), (0, Sp - S), (0, 0), (0, 0))).reshape(Bsz, L, dilation, H, hd)
        return t.transpose(0, 2, 3, 1, 4).reshape(Bsz, dilation, H, nb, BLOCK, hd)

    def with_prev(t):
        prev = jnp.pad(t, ((0, 0), (0, 0), (0, 0), (1, 0), (0, 0), (0, 0)))[:, :, :, :-1]
        return jnp.concatenate([prev, t], axis=4)

    qs = streams(q)
    kb, vb = with_prev(streams(k)), with_prev(streams(v))
    s = jnp.einsum('brhnqd,brhnkd->brhnqk', qs, kb).astype(f32) * (hd ** -0.5)
    qi = jnp.arange(BLOCK)[:, None]
    kj = jnp.arange(2 * BLOCK)[None, :]
    dist = BLOCK + qi - kj
    band = (dist >= 0) & (dist <= n_keys)
    has_prev = (jnp.arange(nb) > 0)[:, None, None] | (kj >= BLOCK)[None]
    mask = band[None] & has_prev
    s = jnp.where(mask, s, NEG)
    lse = jax.nn.logsumexp(s, axis=-1)
    p = jnp.exp(s - lse[..., None])
    o = jnp.einsum('brhnqk,brhnkd->brhnqd', p.astype(v.dtype), vb)
    o = o.reshape(Bsz, dilation, H, L, hd).transpose(0, 3, 1, 2, 4).reshape(Bsz, Sp, H, hd)[:, :S]
    lse = lse.reshape(Bsz, dilation, H, L).transpose(0, 3, 1, 2).reshape(Bsz, Sp, H)[:, :S]
    return o, lse

def dilated_attention(q, k, v):
    outs, lses = [], []
    for window, dilation in DIL_PATTERNS:
        o, lse = dilated_pattern(q, k, v, window, dilation)
        outs.append(o)
        lses.append(lse)
    wts = jax.nn.softmax(jnp.stack(lses), axis=0)
    return jnp.einsum('pbsh,pbshd->bshd', wts.astype(q.dtype), jnp.stack(outs))

def rotate(x):
    S, half = x.shape[1], x.shape[-1] // 2
    inv = 1.0 / (ROT_BASE ** jnp.linspace(0.0, 1.0, half, dtype=f32))
    ang = jnp.arange(S, dtype=f32)[:, None] * inv[None, :]
    cos, sin = jnp.cos(ang)[None, :, None, :], jnp.sin(ang)[None, :, None, :]
    x1, x2 = x[..., 0::2].astype(f32), x[..., 1::2].astype(f32)
    y = jnp.stack([x1 * cos - x2 * sin, x1 * sin + x2 * cos], axis=-1)
    return y.reshape(x.shape).astype(x.dtype)

def retention(q, k, v):
    Bsz, S, H, dk = q.shape
    dv = v.shape[-1]
    C = RET_CHUNK
    nC = S // C
    log_gamma = jnp.log1p(-jnp.power(2.0, -5.0 - jnp.arange(H, dtype=f32)))
    pos = jnp.arange(C, dtype=f32)
    rel = pos[:, None] - pos[None, :]
    intra = jnp.where(rel >= 0, jnp.exp(log_gamma[:, None, None] * jnp.maximum(rel, 0.0)), 0.0)
    chunks = lambda t: t.reshape(Bsz, nC, C, H, t.shape[-1]).transpose(1, 0, 3, 2, 4)
    qc, kc, vc = chunks(q), chunks(k), chunks(v)
    s = jnp.einsum('nbhqd,nbhkd->nbhqk', qc, kc).astype(f32) * intra
    inner = jnp.einsum('nbhqk,nbhkd->nbhqd', s.astype(v.dtype), vc).astype(f32)
    q_decay = jnp.exp(log_gamma[:, None] * (pos + 1.0))[None, :, :, None]
    k_decay = jnp.exp(log_gamma[:, None] * (C - 1.0 - pos))[None, :, :, None]
    chunk_decay = jnp.exp(log_gamma * C)[None, :, None, None]

    def step(state, inp):
        q_i, k_i, v_i = inp
        cross = jnp.einsum('bhqd,bhde->bhqe', q_i.astype(f32), state) * q_decay
        state = state * chunk_decay + jnp.einsum('bhkd,bhke->bhde', k_i.astype(f32) * k_decay, v_i.astype(f32))
        return state, cross

    _, cross = lax.scan(step, jnp.zeros((Bsz, H, dk, dv), f32), (qc, kc, vc))
    out = inner + cross
    return out.transpose(1, 0, 3, 2, 4).reshape(Bsz, S, H, dv)

def head_group_norm(y):
    mu = jnp.mean(y, axis=-1, keepdims=True)
    var = jnp.mean(jnp.square(y - mu), axis=-1, keepdims=True)
    return (y - mu) * lax.rsqrt(var + EPS)

def even_layer(x, g_norm, w_in, b_f, w_out):
    Bsz, S, _ = x.shape
    z = rms_norm(x, g_norm) @ w_in
    cuts = [WIDTH_FOX, 2 * WIDTH_FOX, 3 * WIDTH_FOX, 4 * WIDTH_FOX,
            4 * WIDTH_FOX + N_HEADS_FOX,
            4 * WIDTH_FOX + N_HEADS_FOX + WIDTH_DIL,
            4 * WIDTH_FOX + N_HEADS_FOX + 2 * WIDTH_DIL,
            4 * WIDTH_FOX + N_HEADS_FOX + 3 * WIDTH_DIL]
    qa, ka, va, ga, fa, qb, kb, vb, gb = jnp.split(z, cuts, axis=-1)
    hA = lambda t: t.reshape(Bsz, S, N_HEADS_FOX, HEAD_DIM)
    hB = lambda t: t.reshape(Bsz, S, N_HEADS_DIL, HEAD_DIM)
    log_f = jax.nn.log_sigmoid(fa.astype(f32) + b_f.astype(f32))
    ya = forgetting_attention(hA(qa), hA(ka), hA(va), log_f).reshape(Bsz, S, WIDTH_FOX)
    yb = dilated_attention(hB(qb), hB(kb), hB(vb)).reshape(Bsz, S, WIDTH_DIL)
    y = jnp.concatenate([ya * jax.nn.silu(ga), yb * jax.nn.silu(gb)], axis=-1)
    return x + y @ w_out

def odd_layer(x, g_norm, w_in, w_out):
    Bsz, S, _ = x.shape
    qk_w, v_w = N_HEADS_RET * RET_QK_DIM, N_HEADS_RET * RET_V_DIM
    z = rms_norm(x, g_norm) @ w_in
    q, k, v, g = jnp.split(z, [qk_w, 2 * qk_w, 2 * qk_w + v_w], axis=-1)
    q = rotate(q.reshape(Bsz, S, N_HEADS_RET, RET_QK_DIM))
    k = rotate(k.reshape(Bsz, S, N_HEADS_RET, RET_QK_DIM)) * (RET_QK_DIM ** -0.5)
    y = retention(q, k, v.reshape(Bsz, S, N_HEADS_RET, RET_V_DIM))
    y = head_group_norm(y).reshape(Bsz, S, v_w).astype(x.dtype)
    return x + (y * jax.nn.silu(g)) @ w_out

def first_inputs(seed: int = 0) -> dict:
    key = jax.random.key(seed)
    ks = jax.random.split(key, 12)
    x = jax.random.normal(ks[0], (BATCH, SEQ, D_MODEL), f32)
    even_norm = 1.0 + 0.02 * jax.random.normal(ks[1], (N_EVEN, D_MODEL), f32)
    even_w_in = jax.random.normal(ks[2], (N_EVEN, D_MODEL, EVEN_IN), f32) * D_MODEL ** -0.5
    even_b_f = jax.random.uniform(ks[3], (N_EVEN, N_HEADS_FOX), f32, 1.0, 5.0)
    even_w_out = jax.random.normal(ks[4], (N_EVEN, EVEN_MIX, D_MODEL), f32) * EVEN_MIX ** -0.5
    odd_norm = 1.0 + 0.02 * jax.random.normal(ks[5], (N_ODD, D_MODEL), f32)
    odd_w_in = jax.random.normal(ks[6], (N_ODD, D_MODEL, ODD_IN), f32) * D_MODEL ** -0.5
    odd_w_out = jax.random.normal(ks[7], (N_ODD, ODD_MIX, D_MODEL), f32) * ODD_MIX ** -0.5
    final_norm = 1.0 + 0.02 * jax.random.normal(ks[8], (D_MODEL,), f32)
    return {"x": x, "even_norm": even_norm, "even_w_in": even_w_in, "even_b_f": even_b_f,
            "even_w_out": even_w_out, "odd_norm": odd_norm, "odd_w_in": odd_w_in,
            "odd_w_out": odd_w_out, "final_norm": final_norm}

def first_block(x, even_norm, even_w_in, even_b_f, even_w_out, odd_norm, odd_w_in, odd_w_out, final_norm):
    for layer in range(DEPTH):
        j = layer // 2
        if layer % 2 == 0:
            x = even_layer(x, even_norm[j], even_w_in[j], even_b_f[j], even_w_out[j])
        else:
            x = odd_layer(x, odd_norm[j], odd_w_in[j], odd_w_out[j])
    return rms_norm(x, final_norm)


DEPTH_2 = 1

MIX_WIDTH = D_MODEL
SSM_WIDTH = MIX_WIDTH // 2
SSM_GROUP = 16
SSM_GROUPS = SSM_WIDTH // SSM_GROUP
SSM_STATE = 64
ATTN_WIDTH = MIX_WIDTH - SSM_WIDTH
N_Q_HEADS = ATTN_WIDTH // HEAD_DIM
N_KV_HEADS = 2
Q_PER_KV = N_Q_HEADS // N_KV_HEADS
KV_WIDTH = N_KV_HEADS * HEAD_DIM
IN_WIDTH = SSM_WIDTH + ATTN_WIDTH + 2 * KV_WIDTH
WINDOW = 128
ROPE_DIM = HEAD_DIM // 4
ROPE_THETA = 500000.0
D_FF = -(-8 * D_MODEL // (3 * 256)) * 256
NORM_EPS = 1e-6
DT_MIN = 1e-3
DT_MAX = 1e-1
MASK_VALUE = -1e30


def rms_norm_2(x, g):
    xf = x.astype(jnp.float32)
    y = xf * lax.rsqrt(jnp.mean(xf * xf, axis=-1, keepdims=True) + NORM_EPS)
    return (y * g.astype(jnp.float32)).astype(x.dtype)

def _s5_combine(e1, e2):
    a1r, a1i, b1r, b1i = e1
    a2r, a2i, b2r, b2i = e2
    ar = a2r * a1r - a2i * a1i
    ai = a2r * a1i + a2i * a1r
    br = a2r * b1r - a2i * b1i + b2r
    bi = a2r * b1i + a2i * b1r + b2i
    return (ar, ai, br, bi)

def s5_mixer(u, lam_re, lam_im, log_dt, b_re, b_im, c_re, c_im, d, w_glu, b_glu):
    bsz, L, _ = u.shape
    uf = u.astype(jnp.float32).reshape(bsz, L, SSM_GROUPS, SSM_GROUP)
    lr = jnp.minimum(lam_re.astype(jnp.float32), -1e-4)
    li = lam_im.astype(jnp.float32)
    dt = jnp.exp(log_dt.astype(jnp.float32))[:, None]
    mag = jnp.exp(lr * dt)
    ar = mag * jnp.cos(li * dt)
    ai = mag * jnp.sin(li * dt)
    den = lr * lr + li * li
    fr = ((ar - 1.0) * lr + ai * li) / den
    fi = (ai * lr - (ar - 1.0) * li) / den
    br = b_re.astype(jnp.float32)
    bi = b_im.astype(jnp.float32)
    bbar_re = fr[..., None] * br - fi[..., None] * bi
    bbar_im = fr[..., None] * bi + fi[..., None] * br
    bu_re = jnp.einsum('blgh,gph->blgp', uf, bbar_re)
    bu_im = jnp.einsum('blgh,gph->blgp', uf, bbar_im)
    a_re = jnp.broadcast_to(ar, (1, L, SSM_GROUPS, SSM_STATE))
    a_im = jnp.broadcast_to(ai, (1, L, SSM_GROUPS, SSM_STATE))
    _, _, xr, xi = lax.associative_scan(_s5_combine, (a_re, a_im, bu_re, bu_im), axis=1)
    y = (jnp.einsum('blgp,ghp->blgh', xr, c_re.astype(jnp.float32))
         - jnp.einsum('blgp,ghp->blgh', xi, c_im.astype(jnp.float32))
         + d.astype(jnp.float32) * uf)
    y = jax.nn.gelu(y.reshape(bsz, L, SSM_WIDTH))
    z = y @ w_glu.astype(jnp.float32) + b_glu.astype(jnp.float32)
    out = z[..., :SSM_WIDTH] * jax.nn.sigmoid(z[..., SSM_WIDTH:])
    return out.astype(u.dtype)

def partial_rotary(t, positions):
    half = ROPE_DIM // 2
    inv_freq = ROPE_THETA ** (-jnp.arange(half, dtype=jnp.float32) * 2.0 / ROPE_DIM)
    ang = positions.astype(jnp.float32)[..., None] * inv_freq
    cos = jnp.cos(ang)[:, :, None, :]
    sin = jnp.sin(ang)[:, :, None, :]
    tf = t.astype(jnp.float32)
    t1 = tf[..., :half]
    t2 = tf[..., half:ROPE_DIM]
    rot = jnp.concatenate([t1 * cos - t2 * sin, t2 * cos + t1 * sin, tf[..., ROPE_DIM:]], axis=-1)
    return rot.astype(t.dtype)

def sliding_window_sink_attention(q, k, v, sinks):
    bsz, L = q.shape[0], q.shape[1]
    nb = L // BLOCK
    qb = q.reshape(bsz, nb, BLOCK, N_KV_HEADS, Q_PER_KV, HEAD_DIM).transpose(1, 0, 2, 3, 4, 5)

    def windows(t):
        tb = t.reshape(bsz, nb, BLOCK, N_KV_HEADS, HEAD_DIM)
        prev = jnp.pad(tb, ((0, 0), (1, 0), (0, 0), (0, 0), (0, 0)))[:, :-1]
        return jnp.concatenate([prev, tb], axis=2).transpose(1, 0, 2, 3, 4)

    kw = windows(k)
    vw = windows(v)
    qi = jnp.arange(BLOCK)[:, None]
    kj = jnp.arange(2 * BLOCK)[None, :]
    rel = qi + BLOCK - kj
    band = (rel >= 0) & (rel < WINDOW)
    sink = sinks.astype(jnp.float32).reshape(N_KV_HEADS, Q_PER_KV)[None, :, :, None, None]
    scale = HEAD_DIM ** -0.5

    def one_block(args):
        q_blk, k_blk, v_blk, blk = args
        valid = band & (blk * BLOCK - BLOCK + kj >= 0)
        s = jnp.einsum('bqhgd,bkhd->bhgqk', q_blk, k_blk).astype(jnp.float32) * scale
        s = jnp.where(valid, s, MASK_VALUE)
        m = jnp.maximum(jnp.max(s, axis=-1, keepdims=True), sink)
        p = jnp.exp(s - m)
        p = p / (jnp.sum(p, axis=-1, keepdims=True) + jnp.exp(sink - m))
        return jnp.einsum('bhgqk,bkhd->bqhgd', p.astype(v_blk.dtype), v_blk)

    o = lax.map(one_block, (qb, kw, vw, jnp.arange(nb)))
    return o.transpose(1, 0, 2, 3, 4, 5).reshape(bsz, L, ATTN_WIDTH)

def second_inputs(seed: int = 0) -> dict:
    key = jax.random.key(seed)
    ks = jax.random.split(key, 24)
    f32 = jnp.float32

    def nrm(k, shape, std):
        return jax.random.normal(k, shape, f32) * std

    def gain(k, n):
        return 1.0 + 0.05 * jax.random.normal(k, (DEPTH_2, n), f32)

    n_idx = jnp.arange(SSM_STATE, dtype=f32)
    lam_re = -0.5 + 0.01 * jax.random.normal(ks[3], (DEPTH_2, SSM_GROUPS, SSM_STATE), f32)
    lam_im = math.pi * n_idx + 0.01 * jax.random.normal(ks[4], (DEPTH_2, SSM_GROUPS, SSM_STATE), f32)
    log_dt = jax.random.uniform(ks[5], (DEPTH_2, SSM_GROUPS), f32, math.log(DT_MIN), math.log(DT_MAX))
    return {
        "x": jax.random.normal(ks[0], (BATCH, SEQ, D_MODEL), f32),
        "positions": jnp.broadcast_to(jnp.arange(SEQ, dtype=jnp.int32), (BATCH, SEQ)),
        "g_pre_mix": gain(ks[1], D_MODEL),
        "w_in": nrm(ks[2], (DEPTH_2, D_MODEL, IN_WIDTH), D_MODEL ** -0.5),
        "ssm_lambda_re": lam_re,
        "ssm_lambda_im": lam_im,
        "ssm_log_dt": log_dt,
        "ssm_b_re": nrm(ks[6], (DEPTH_2, SSM_GROUPS, SSM_STATE, SSM_GROUP), (2 * SSM_GROUP) ** -0.5),
        "ssm_b_im": nrm(ks[7], (DEPTH_2, SSM_GROUPS, SSM_STATE, SSM_GROUP), (2 * SSM_GROUP) ** -0.5),
        "ssm_c_re": nrm(ks[8], (DEPTH_2, SSM_GROUPS, SSM_GROUP, SSM_STATE), (2 * SSM_STATE) ** -0.5),
        "ssm_c_im": nrm(ks[9], (DEPTH_2, SSM_GROUPS, SSM_GROUP, SSM_STATE), (2 * SSM_STATE) ** -0.5),
        "ssm_d": nrm(ks[10], (DEPTH_2, SSM_GROUPS, SSM_GROUP), 1.0),
        "w_glu": nrm(ks[11], (DEPTH_2, SSM_WIDTH, 2 * SSM_WIDTH), SSM_WIDTH ** -0.5),
        "b_glu": nrm(ks[12], (DEPTH_2, 2 * SSM_WIDTH), 0.01),
        "attn_sinks": nrm(ks[13], (DEPTH_2, N_Q_HEADS), 0.5),
        "g_ssm_out": gain(ks[14], SSM_WIDTH),
        "g_attn_out": gain(ks[15], ATTN_WIDTH),
        "w_out": nrm(ks[16], (DEPTH_2, MIX_WIDTH, D_MODEL), MIX_WIDTH ** -0.5),
        "g_post_mix": gain(ks[17], D_MODEL),
        "g_pre_ffn": gain(ks[18], D_MODEL),
        "w_gate_up": nrm(ks[19], (DEPTH_2, D_MODEL, 2 * D_FF), D_MODEL ** -0.5),
        "w_down": nrm(ks[20], (DEPTH_2, D_FF, D_MODEL), D_FF ** -0.5),
        "g_post_ffn": gain(ks[21], D_MODEL),
    }

def second_block(x, positions, g_pre_mix, w_in, ssm_lambda_re, ssm_lambda_im, ssm_log_dt,
              ssm_b_re, ssm_b_im, ssm_c_re, ssm_c_im, ssm_d, w_glu, b_glu, attn_sinks,
              g_ssm_out, g_attn_out, w_out, g_post_mix, g_pre_ffn, w_gate_up, w_down, g_post_ffn):
    bsz, L, _ = x.shape
    h = x
    for l in range(DEPTH_2):
        hn = rms_norm_2(h, g_pre_mix[l])
        proj = hn @ w_in[l]
        u = proj[..., :SSM_WIDTH]
        q = proj[..., SSM_WIDTH:SSM_WIDTH + ATTN_WIDTH]
        k = proj[..., SSM_WIDTH + ATTN_WIDTH:SSM_WIDTH + ATTN_WIDTH + KV_WIDTH]
        v = proj[..., SSM_WIDTH + ATTN_WIDTH + KV_WIDTH:]

        y_ssm = s5_mixer(u, ssm_lambda_re[l], ssm_lambda_im[l], ssm_log_dt[l],
                         ssm_b_re[l], ssm_b_im[l], ssm_c_re[l], ssm_c_im[l], ssm_d[l],
                         w_glu[l], b_glu[l])

        q = partial_rotary(q.reshape(bsz, L, N_Q_HEADS, HEAD_DIM), positions)
        k = partial_rotary(k.reshape(bsz, L, N_KV_HEADS, HEAD_DIM), positions)
        v = v.reshape(bsz, L, N_KV_HEADS, HEAD_DIM)
        y_attn = sliding_window_sink_attention(q, k, v, attn_sinks[l])

        merged = jnp.concatenate([rms_norm_2(y_ssm, g_ssm_out[l]), rms_norm_2(y_attn, g_attn_out[l])], axis=-1)
        h = h + rms_norm_2(merged @ w_out[l], g_post_mix[l])

        hn = rms_norm_2(h, g_pre_ffn[l])
        gu = hn @ w_gate_up[l]
        ff = (jax.nn.silu(gu[..., :D_FF]) * gu[..., D_FF:]) @ w_down[l]
        h = h + rms_norm_2(ff, g_post_ffn[l])
    return h


def setup_inputs(seed=0):
    out = dict(first_inputs(seed))
    for name, value in second_inputs(seed + 1).items():
        if name != "x":
            out[name + "_2"] = value
    return out


def reference(
    x, even_norm, even_w_in, even_b_f, even_w_out, odd_norm, odd_w_in, odd_w_out, final_norm,
    positions_2, g_pre_mix_2, w_in_2, ssm_lambda_re_2, ssm_lambda_im_2, ssm_log_dt_2,
    ssm_b_re_2, ssm_b_im_2, ssm_c_re_2, ssm_c_im_2, ssm_d_2, w_glu_2, b_glu_2, attn_sinks_2,
    g_ssm_out_2, g_attn_out_2, w_out_2, g_post_mix_2, g_pre_ffn_2, w_gate_up_2, w_down_2,
    g_post_ffn_2,
):
    x = first_block(
        x, even_norm, even_w_in, even_b_f, even_w_out, odd_norm, odd_w_in, odd_w_out,
        final_norm,
    )
    return second_block(
        x, positions_2, g_pre_mix_2, w_in_2, ssm_lambda_re_2, ssm_lambda_im_2, ssm_log_dt_2,
        ssm_b_re_2, ssm_b_im_2, ssm_c_re_2, ssm_c_im_2, ssm_d_2, w_glu_2, b_glu_2, attn_sinks_2,
        g_ssm_out_2, g_attn_out_2, w_out_2, g_post_mix_2, g_pre_ffn_2, w_gate_up_2, w_down_2,
        g_post_ffn_2,
    )


_drawn_inputs = setup_inputs


def setup_inputs(seed=0):
    import zlib

    import numpy as np

    out = dict(_drawn_inputs(seed))
    spreads = {}
    factors = {'even_norm': 4.076,
     'ssm_lambda_re_2': 200.0,
     'b_glu_2': 5.949,
     'attn_sinks_2': 4.355,
     'odd_norm': 8.0,
     'ssm_lambda_im_2': 34.712,
     'ssm_log_dt_2': 36.872,
     'ssm_b_re_2': 47.72,
     'ssm_b_im_2': 48.4,
     'ssm_c_re_2': 48.368,
     'ssm_c_im_2': 48.184}
    for name, (base, spread) in spreads.items():
        noise = np.random.default_rng([zlib.crc32(name.encode()), seed]).standard_normal(out[name].shape)
        drawn = base * np.exp(spread * noise) if base else spread * noise
        out[name] = __import__('jax').numpy.asarray(drawn.astype(out[name].dtype))
    for name, factor in factors.items():
        out[name] = (out[name] * factor).astype(out[name].dtype)
    return out
```

```python
from contextlib import ExitStack

import numpy as np

import concourse.bass as bass
from concourse import mybir

F32 = mybir.dt.float32
F32R = mybir.dt.float32r
I32 = mybir.dt.int32
ACT = mybir.ActivationFunctionType
ALU = mybir.AluOpType

P = 128
S = 256
NB = S // P
D = 1024
KD = D // P
HD = 64
FOX_H = DIL_H = 16
EVEN_W = 1024
RET_H, RET_QK, RET_V = 4, 256, 512
SSM_W, SSM_G, SSM_N, SSM_C = 512, 32, 64, 16
ST = SSM_G * SSM_N // P
CT = SSM_W // P
SINK_H, KV_H = 8, 2
DFF = 2816
KF = DFF // P
ROPE_HALF = 8
EPS = 1e-6
NEG = 1e30
BANK = 512

RING = 4
UNIT = 1024
AHEAD = 3

PI = float(np.float32(np.pi))
TWO_PI_1 = 6.28125
TWO_PI_2 = float(np.float32(np.float32((2 * np.pi - TWO_PI_1) * 2**21).round() / 2**21))
TWO_PI_3 = float(np.float32(2 * np.pi - TWO_PI_1 - TWO_PI_2))
INV_2PI = float(np.float32(1 / (2 * np.pi)))
ROUND_INT = 1.5 * 2.0**23
ROUND_13 = 1.5 * 2.0**10


def constant_tables():
    q = np.arange(P)[:, None]
    far, near = P + q - np.arange(P)[None], q - np.arange(P)[None]
    dist = np.concatenate([far, near], 1)
    causal = np.where(dist >= 0, 0.0, NEG)
    times = ((dist >= 0) & (dist <= 128)).astype(int) + ((dist >= 0) & (dist % 4 == 0)) + ((dist >= 0) & (dist % 16 == 0))
    dilated = np.where(times > 0, -np.log(np.maximum(times, 1)), NEG)
    window = np.where((dist >= 0) & (dist < 128), 0.0, NEG)
    neg_bias = np.stack([causal, dilated, window], 1)
    tri = (np.arange(P)[:, None] <= np.arange(P)[None]).astype(np.float64)
    prefix = np.stack([np.concatenate([tri, np.ones((P, P))], 1), np.concatenate([np.zeros((P, P)), tri], 1)], 1)
    half = RET_QK // 2
    inv = 1.0 / (np.float32(10000.0) ** np.linspace(0.0, 1.0, half, dtype=np.float32))
    ang = (np.arange(S, dtype=np.float32)[None] * inv.astype(np.float32)[:, None]).astype(np.float32)
    rot = np.stack([np.cos(ang), np.sin(ang)], 1)
    log_gamma = np.log1p(-(2.0 ** (-5.0 - np.arange(RET_H))))
    lag = np.arange(S)[None] - np.arange(P)[:, None]
    decay = np.where(lag[:, None] >= 0, np.exp(log_gamma[None, :, None] * np.maximum(lag, 0)[:, None]), 0.0) * RET_QK**-0.5
    inv_freq = np.float32(500000.0) ** (-np.arange(ROPE_HALF, dtype=np.float32) * np.float32(2.0 / 16))
    group_parity = (np.arange(P)[:, None] // SSM_C % 2 == np.arange(2)[None])
    steps = np.broadcast_to(np.arange(S)[None], (P, S))
    f = lambda a: np.ascontiguousarray(a, dtype=np.float32)
    return {
        "ident": f(np.eye(P)), "neg_bias": f(neg_bias), "prefix": f(prefix), "rot": f(rot), "decay": f(decay),
        "inv_freq": f(np.broadcast_to(inv_freq[None], (P, ROPE_HALF))), "parity": f(group_parity), "steps": f(steps),
    }


def weight_chunks():
    table, unit = {}, 0

    def add(name, units, per_unit):
        nonlocal unit
        table[name] = (unit, units, per_unit, len(table))
        unit += units

    for name in ("ga", "gb", "qa", "ka", "va", "qb", "kb", "vb"):
        for c in range(2):
            add((name, c), KD // 2, 2)
    for c in range(2):
        add(("even_out", c), 2 * KD // 2, 2)
    for name, n in (("rq", 2), ("rk", 2), ("rv", 4), ("rg", 4)):
        for c in range(n):
            add((name, c), KD // 2, 2)
    for c in range(2):
        add(("odd_out", c), RET_H * RET_V // P // 2, 2)
    add(("u", 0), KD // 2, 2)
    add(("sq", 0), KD // 2, 2)
    add(("skv", 0), 2, 4)
    for c in range(2):
        add(("glu", c), SSM_W // P // 2, 2)
    for c in range(2):
        add(("mix_out", c), KD // 2, 2)
    for c in range(DFF // 256):
        add(("ffn", c), 4, 4)
    for c in range(2):
        add(("down", c), KF // 2, 2)
    return table, unit


def build(nc, t):
    chunks, n_units = weight_chunks()
    number = {name: c[3] for name, c in chunks.items()}
    last_unit = {name: c[0] + c[1] - 1 for name, c in chunks.items()}

    with ExitStack() as ctx:
        sem = lambda name: ctx.enter_context(nc.semaphore(name))
        sb = lambda name, shape, dt=F32: ctx.enter_context(nc.sbuf_tensor(name, shape, dt))

        stage = sb("stage", [P, RING, UNIT])
        w_hi = sb("w_hi", [P, RING, UNIT], F32R)
        w_lo = sb("w_lo", [P, RING, UNIT], F32R)
        x = sb("x", [P, NB, D])
        act_t = sb("act_t", [P, 16, S], F32R)
        prob = sb("prob", [P, 3, 384])
        prob_t = sb("prob_t", [P, 2, 384])
        cos_t = sb("cos_t", [P, ST, S])
        sin_t = sb("sin_t", [P, ST, S])
        forget_bias = cos_t[:, 0:FOX_H, :]
        forget_bias0 = sin_t[:, :, :].rearrange("p a b -> p (a b)")[:, 0:FOX_H * P].rearrange("p (h k) -> p h k", h=FOX_H)
        wave_k, wave_part = sb("wave_k", [P, 2, S]), sb("wave_part", [P, 2, S])
        b_re, b_im = sb("b_re", [P, CT, P]), sb("b_im", [P, CT, P])
        c_re, c_re_neg, c_im_neg = sb("c_re", [P, CT, P]), sb("c_re_neg", [P, CT, P]), sb("c_im_neg", [P, CT, P])
        row_a, row_b = sb("row_a", [P, D]), sb("row_b", [P, D])
        ident = sb("ident", [P, P])
        neg_bias = sb("neg_bias", [P, 3, S])
        prefix = sb("prefix", [P, NB, S])
        rot = sb("rot", [P, 2, S])
        decay = sb("decay", [P, RET_H, S])
        steps = sb("steps", [P, S])
        inv_freq, parity = sb("inv_freq", [P, ROPE_HALF]), sb("parity", [P, 2])
        N_ROWS = 4 * KD + 3 * CT + 2 * ST
        rows = sb("rows", [P, P])
        col = sb("col", [P, N_ROWS])
        COL_EVEN, COL_ODD, COL_MIX, COL_FFN = 0, KD, 2 * KD, 3 * KD
        COL_GSSM, COL_GATTN, COL_SKIP = 4 * KD, 4 * KD + CT, 4 * KD + 2 * CT
        COL_LRE = 4 * KD + 3 * CT
        COL_LIM = COL_LRE + ST
        sumsq, rstd = sb("sumsq", [P, 18]), sb("rstd", [P, 18])
        neg_half, half_pi = sb("neg_half", [P, 8]), sb("half_pi", [P, 1])
        wf = sb("wf", [P, KD, FOX_H])
        wf_hi, wf_lo = sb("wf_hi", [P, KD, FOX_H], F32R), sb("wf_lo", [P, KD, FOX_H], F32R)
        bf = sb("bf", [P, FOX_H])
        gate_f = sb("gate_f", [P, 4, NB, FOX_H])
        cum_t = sb("cum_t", [FOX_H, S])
        N_HEADS = FOX_H + DIL_H + SINK_H
        neg_max, den, inv_den = sb("neg_max", [P, NB, N_HEADS]), sb("den", [P, NB, N_HEADS]), sb("inv_den", [P, NB, N_HEADS])
        sink, neg_sink, sink_exp = sb("sink", [P, SINK_H]), sb("neg_sink", [P, SINK_H]), sb("sink_exp", [P, NB, SINK_H])
        log_dt = sb("log_dt", [P, SSM_G])
        pos_i, pos = sb("pos_i", [P, NB], I32), sb("pos", [P, NB])
        NA = ST + NB * ROPE_HALF
        sm = {n: sb("sm_" + n, [P, NA]) for n in ("ang", "k", "r", "sin", "cos", "abs")}
        sp = {n: sb("sp_" + n, [P, ST]) for n in ("lre", "ldt", "dt", "mdt", "mag", "ar", "ai", "den", "t", "fr", "fi", "hi", "lo")}
        stats, mean_var, ret_rstd = sb("stats", [P, NB, 6]), sb("mean_var", [P, RET_H, NB, 2]), sb("ret_rstd", [P, RET_H, NB])

        WORK = 12288
        sb("work", [P, WORK])
        work_from = nc.sbuf_base - 4 * WORK

        def over(name, at, shape, dt=F32):
            return nc.alloc_sbuf_tensor_at(name, shape, dt, offset=work_from + 4 * at)

        xs = over("xs", 10240, [P, NB, D])
        q0, k0, v0 = over("q0", 0, [P, 8, S]), over("k0", 2048, [P, 8, S]), over("v0", 4096, [P, NB, 1024])
        gate0 = [over("gate_a", 6144, [P, NB, 1024]), over("gate_b", 8192, [P, NB, 1024])]
        b_in = [over("b_in_re", 10240, [P, ST, SSM_C]), over("b_in_im", 10496, [P, ST, SSM_C])]
        b_tmp = [over("b_tmp0", 10752, [P, ST, SSM_C]), over("b_tmp1", 11008, [P, ST, SSM_C])]
        b_wide = [over("b_wide_re", 11264, [P, ST, 2, SSM_C]), over("b_wide_im", 11776, [P, ST, 2, SSM_C])]
        c_in = [sb("c_in_re", [P, CT, SSM_N]), sb("c_in_im", [P, CT, SSM_N])]
        c_wide = [prob[:, :, :].rearrange("p a b -> p (a b)")[:, 0:512], prob[:, :, :].rearrange("p a b -> p (a b)")[:, 512:1024]]
        y_lo = over("y_lo", 0, [P, 16, S], F32R)
        q1, k1 = over("q1", 0, [P, RET_H, 2, S]), over("k1", 2048, [P, RET_H, 2, S])
        v1, gate1 = over("v1", 4096, [P, NB, 2048]), over("gate1", 8192, [P, NB, 2048])
        u_t = over("u_t", 0, [P, CT, S])
        qkv = over("qkv", 1024, [P, NB, 12, HD])
        k_twice = over("k_twice", 2560, [P, NB, KV_H, 2, HD])
        q_t, k_t = over("q_t", 3072, [P, 4, S]), over("k_t", 4096, [P, KV_H, S])
        y_attn = over("y_attn", 4608, [P, NB, 512])
        gelu_hi, gelu_lo = over("gelu_hi", 5632, [P, CT, S], F32R), over("gelu_lo", 6656, [P, CT, S], F32R)
        ssm_a, ssm_b = over("ssm_a", 8192, [P, 3, 512]), over("ssm_b", 9728, [P, 3, 512])
        y_ssm = over("y_ssm", 11264, [P, CT, S])
        ssm_out, gate_z = over("ssm_out", 1024, [P, NB, 512]), over("gate_z", 2048, [P, NB, 512])
        rope_tmp = over("rope_tmp", 7680, [P, 1, 512])
        mixed = over("mixed", 4608, [P, NB, D])
        ff_hi, ff_lo = over("ff_hi", 0, [P, KF, S], F32R), over("ff_lo", 5632, [P, KF, S], F32R)
        down_out, down_junk = (w[:, 0:8, :].rearrange("p (b k) n -> p b (k n)", b=NB) for w in (cos_t, sin_t))
        ff_tmp = [prob[:, :, :].rearrange("p a b -> p (a b)")[:, 0:512], prob[:, :, :].rearrange("p a b -> p (a b)")[:, 512:1024]]
        ff_val = [prob_t[:, :, :].rearrange("p a b -> p (a b)")[:, 0:512]]

        ps = ctx.enter_context(nc.psum_tensor("ps", [P, 8 * BANK], F32))

        def bank(b, width=BANK, at=0):
            return ps[:, b * BANK + at:b * BANK + at + width]

        landed = [sem(f"unit_landed_{i}") for i in range(RING)]
        hi_ready, lo_ready, unit_used = sem("hi_ready"), sem("lo_ready"), sem("unit_used")
        drained = [sem("chunk_drained_even"), sem("chunk_drained_odd")]
        x_in, rows_in, tables_in, params_in = sem("x_in"), sem("rows_in"), sem("tables_in"), sem("params_in")
        row_a_in, row_b_in, out_stored = sem("row_a_in"), sem("row_b_in"), sem("out_stored")
        fills = sem("fills")
        squared, var_ready, rstd_ready, xs_ready = sem("squared"), sem("var_ready"), sem("rstd_ready"), sem("xs_ready")
        turned, act_hi, act_lo = sem("turned"), sem("act_hi"), sem("act_lo")
        x_ready, h_ready = sem("x_ready"), sem("h_ready")
        dve_step, act_step, pool_step = sem("dve_step"), sem("act_step"), sem("pool_step")
        col_turned, col_ready = sem("col_turned"), sem("col_ready")
        ldt_ready, dt_ready, mdt_ready, mag_ready = sem("ldt_ready"), sem("dt_ready"), sem("mdt_ready"), sem("mag_ready")
        ang_ready, trig_ready = sem("ang_ready"), sem("trig_ready")
        b_wide_ready, b_turned, b_ready = sem("b_wide_ready"), sem("b_turned"), sem("b_ready")
        c_wide_ready, c_turned, c_ready = sem("c_wide_ready"), sem("c_turned"), sem("c_ready")
        wf_hi_ready, wf_lo_ready, f_done, f_abs, f_exp, f_ln, f_ready = (sem(n) for n in ("wf_hi_ready", "wf_lo_ready", "f_done", "f_abs", "f_exp", "f_ln", "f_ready"))
        cum_done, cum_ready = sem("cum_done"), sem("cum_ready")
        cum_stored, cum_spread, forget_bias_ready = sem("cum_stored"), sem("cum_spread"), sem("forget_bias_ready")
        scores, scored, exped, prob_turned, prob_copied, pv_done = (sem(n) for n in ("scores", "scored", "exped", "prob_turned", "prob_copied", "pv_done"))
        inv_ready, gate_scaled, heads_out = sem("inv_ready"), sem("gate_scaled"), sem("heads_out")
        wave_ready, wave_sin = sem("wave_ready"), sem("wave_sin")
        ret_scores, ret_decayed, ret_pv, ret_var, ret_scale, ret_gated, ret_out = (sem(n) for n in ("ret_scores", "ret_decayed", "ret_pv", "ret_var", "ret_scale", "ret_gated", "ret_out"))
        bu_done, bu_read, v_ready, scan_done, prod_ready, y_done, y_added = (sem(n) for n in ("bu_done", "bu_read", "v_ready", "scan_done", "prod_ready", "y_done", "y_added"))
        gelu_hi_ready, gelu_ready, gelu_lo_ready = sem("gelu_hi_ready"), sem("gelu_ready"), sem("gelu_lo_ready")
        rope_ready, k_twice_ready, qk_turned, qk_ready = sem("rope_ready"), sem("k_twice_ready"), sem("qk_turned"), sem("qk_ready")
        sink_ready, sink_sum, sink_exped, y_attn_ready = sem("sink_ready"), sem("sink_sum"), sem("sink_exped"), sem("y_attn_ready")
        sig_ready, ssm_out_ready = sem("sig_ready"), sem("ssm_out_ready")
        silu_ready, ff_ready, ff_hi_ready, ff_lo_ready = sem("silu_ready"), sem("ff_ready"), sem("ff_hi_ready"), sem("ff_lo_ready")

        def result(name, width=BANK):
            n = number[name]
            return ps[:, (n % 2) * 2 * BANK:(n % 2) * 2 * BANK + 2 * BANK].rearrange("p (b n) -> p b n", b=2)[:, :, 0:width]

        def chunk_done(eng, name):
            eng.wait_ge(unit_used, last_unit[name] + 1)

        def chunk_drained(eng, name):
            n = number[name]
            eng.wait_ge(drained[n % 2], n // 2 + 1)

        def drain_sem(name):
            return drained[number[name] % 2]

        w_even = t["even_w_in"].rearrange("(t p) n -> p t n", p=P)
        even_at = {"qa": 0, "ka": 1024, "va": 2048, "ga": 3072, "fa": 4096, "qb": 4112, "kb": 5136, "vb": 6160, "gb": 7184}
        w_even_out = t["even_w_out"].rearrange("(t p) n -> p t n", p=P)
        w_odd = t["odd_w_in"].rearrange("(t p) n -> p t n", p=P)
        odd_at = {"rq": 0, "rk": 1024, "rv": 2048, "rg": 4096}
        w_odd_out = t["odd_w_out"].rearrange("(t p) n -> p t n", p=P)
        w_in = t["w_in_2"].rearrange("(t p) n -> p t n", p=P)
        in_at = {"u": 0, "sq": 512, "skv": 1024}
        w_glu = t["w_glu_2"].rearrange("(t p) n -> p t n", p=P)
        w_mix = t["w_out_2"].rearrange("(t p) n -> p t n", p=P)
        w_gu = t["w_gate_up_2"].rearrange("(t p) n -> p t n", p=P)
        w_down = t["w_down_2"].rearrange("(t p) n -> p t n", p=P)

        def unit_source(name, j):
            kind, c = name
            per = chunks[name][2]
            ks = slice(j * per, (j + 1) * per)
            if kind in even_at:
                return w_even[:, ks, even_at[kind] + c * 512:even_at[kind] + (c + 1) * 512]
            if kind in odd_at:
                return w_odd[:, ks, odd_at[kind] + c * 512:odd_at[kind] + (c + 1) * 512]
            if kind in in_at:
                return w_in[:, ks, in_at[kind]:in_at[kind] + UNIT // per]
            if kind == "ffn":
                at = (j % 2) * DFF + c * 256
                return w_gu[:, (j // 2) * 4:(j // 2 + 1) * 4, at:at + 256]
            w = {"even_out": w_even_out, "odd_out": w_odd_out, "glu": w_glu, "mix_out": w_mix, "down": w_down}[kind]
            return w[:, ks, c * 512:(c + 1) * 512]

        block = ctx.enter_context(nc.Block())

        @block.sync
        def _(sp_eng):
            for name, (first, units, per, _) in chunks.items():
                for j in range(units):
                    u = first + j
                    if u >= RING:
                        sp_eng.wait_ge(lo_ready, u - RING + 1)
                    dst = stage[:, u % RING, :].rearrange("p (t n) -> p t n", t=per)
                    sp_eng.dma_start(dst, unit_source(name, j)).then_inc(landed[u % RING], 16)
            for b in range(NB):
                sp_eng.wait_ge(h_ready, 2 + b + 1)
                sp_eng.dma_start(t["out"][b * P:(b + 1) * P, :], x[:, b, :]).then_inc(out_stored, 16)
            sp_eng.wait_ge(out_stored, 16 * NB)

        @block.gpsimd
        def _(pool):
            n_step = [0]

            def then(ins):
                n_step[0] += 1
                ins.then_inc(pool_step, 1)
                pool.wait_ge(pool_step, n_step[0])

            for dst, src in ((neg_bias[:], t["neg_bias"]), (prefix[:], t["prefix"]), (rot[:], t["rot"]), (decay[:], t["decay"]),
                             (steps[:], t["steps"]), (inv_freq[:], t["inv_freq"]), (parity[:], t["parity"])):
                pool.dma_start(dst, src).then_inc(tables_in, 16)
            pool.dma_start(wf[:], w_even[:, :, even_at["fa"]:even_at["fa"] + FOX_H]).then_inc(params_in, 16)
            pool.dma_start(bf[:], t["even_b_f"].partition_broadcast(P)).then_inc(params_in, 16)
            pool.dma_start(sink[:], t["attn_sinks_2"].partition_broadcast(P)).then_inc(params_in, 16)
            pool.dma_start(log_dt[:], t["ssm_log_dt_2"].partition_broadcast(P)).then_inc(params_in, 16)
            for b in range(NB):
                pool.dma_start(pos_i[:, b:b + 1], t["positions_2"].rearrange("(n o) -> n o", o=1)[b * P:(b + 1) * P, :]).then_inc(params_in, 16)
            for i, name in enumerate(("ssm_c_re_2", "ssm_c_im_2")):
                pool.dma_start(c_in[i][:], t[name].rearrange("(t q) n -> q t n", q=P)).then_inc(params_in, 16)
            pool.dma_start(row_a[:], t["final_norm"].partition_broadcast(P)).then_inc(row_a_in, 16)
            pool.dma_start(row_b[:], t["b_glu_2"].partition_broadcast(P)).then_inc(row_b_in, 16)

            def root(i, width):
                c = slice(2 * i, 2 * i + 2)
                pool.wait_ge(squared, 2 * i + 2)
                then(nc.gpsimd.tensor_scalar(rstd[:, c], sumsq[:, c], 1.0 / width, EPS, ALU.mult, ALU.add))
                nc.gpsimd.tensor_tensor(rstd[:, c], rstd[:, c], neg_half[:, 0:2], ALU.pow).then_inc(rstd_ready, 1)

            pool.wait_ge(fills, 1)
            root(0, D)
            pool.wait_ge(turned, KD)
            for i, name in enumerate(("ssm_b_re_2", "ssm_b_im_2")):
                pool.dma_start(b_in[i][:], t[name].rearrange("(t q) h -> q t h", q=P)).then_inc(params_in, 16)
            then(nc.gpsimd.memset(b_wide[0][:], 0.0))
            nc.gpsimd.memset(b_wide[1][:], 0.0).then_inc(b_wide_ready, 1)
            pool.wait_ge(params_in, 16 * 10)
            pool.wait_ge(tables_in, 16 * 7)
            for i in range(2):
                for a in range(2):
                    dst = c_wide[i].rearrange("p (t a n) -> p t a n", t=CT, a=2)[:, :, a, :]
                    nc.gpsimd.tensor_scalar(dst, c_in[i][:], parity[:, a:a + 1], None, ALU.mult).then_inc(c_wide_ready, 1)

            def scale_gates(g):
                pool.wait_ge(inv_ready, g + 1)
                dst = gate0[g // 2][:, :, (g % 2) * 512:(g % 2) * 512 + 512].rearrange("p b (h d) -> p b h d", d=HD)
                by = inv_den[:, :, 8 * g:8 * g + 8].unsqueeze(3).to_broadcast([P, NB, 8, HD])
                nc.gpsimd.tensor_tensor(dst, dst, by, ALU.mult).then_inc(gate_scaled, 1)

            pool.wait_ge(cum_ready, 1)
            pool.dma_start(t["cum_forget"], cum_t[:]).then_inc(cum_stored, 16)
            pool.wait_ge(cum_stored, 16)
            pool.dma_start(forget_bias, t["cum_forget"].partition_broadcast(P)).then_inc(cum_spread, 16)
            pool.wait_ge(cum_spread, 16)
            for part in range(4):
                hs = slice(4 * part, 4 * part + 4)
                near = neg_bias[:, 0, P:S].unsqueeze(1).to_broadcast([P, 4, P])
                nc.gpsimd.tensor_tensor(forget_bias0[:, hs, :], forget_bias[:, hs, 0:P], near, ALU.add)
                then(nc.gpsimd.tensor_tensor(forget_bias[:, hs, P:S], forget_bias[:, hs, P:S], near, ALU.add))
                far = neg_bias[:, 0, 0:P].unsqueeze(1).to_broadcast([P, 4, P])
                nc.gpsimd.tensor_tensor(forget_bias[:, hs, 0:P], forget_bias[:, hs, 0:P], far, ALU.add).then_inc(forget_bias_ready, 1)

            def waves(i):
                w = slice(2 * i, 2 * i + 2)
                TS, TT = nc.gpsimd.tensor_scalar, nc.gpsimd.tensor_tensor
                ang, r = cos_t[:, w, :], sin_t[:, w, :]
                for s in (2 * i, 2 * i + 1):
                    TS(wave_part[:, s % 2, :], steps[:], sp["lo"][:, s:s + 1], None, ALU.mult)
                    ins = TS(cos_t[:, s, :], steps[:], sp["hi"][:, s:s + 1], None, ALU.mult)
                then(ins)
                then(TS(wave_k[:], ang, INV_2PI, ROUND_INT, ALU.mult, ALU.add))
                then(TS(wave_k[:], wave_k[:], -ROUND_INT, None, ALU.add))
                then(TS(r, wave_k[:], -TWO_PI_1, None, ALU.mult))
                then(TT(ang, ang, r, ALU.add))
                then(TS(r, wave_k[:], -TWO_PI_2, None, ALU.mult))
                then(TT(ang, ang, r, ALU.add))
                then(TS(r, wave_k[:], -TWO_PI_3, None, ALU.mult))
                then(TT(ang, ang, r, ALU.add))
                then(TT(r, ang, wave_part[:], ALU.add))
                TS(r, r, PI, -PI, ALU.min, ALU.max).then_inc(wave_ready, 1)

            scale_gates(0)
            scale_gates(1)
            pool.wait_ge(scored, FOX_H)
            for i in range(3):
                waves(i)
            scale_gates(2)
            scale_gates(3)
            root(1, D)
            for i in range(3, 8):
                waves(i)
            for h in range(RET_H):
                pool.wait_ge(ret_var, h + 1)
                then(nc.gpsimd.tensor_scalar(ret_rstd[:, h, :], mean_var[:, h, :, 1], EPS, None, ALU.add))
                nc.gpsimd.tensor_tensor(ret_rstd[:, h, :], ret_rstd[:, h, :], neg_half[:, 0:2], ALU.pow).then_inc(ret_scale, 1)
            root(2, D)
            pool.wait_ge(h_ready, 2)
            pool.dma_start(row_a[:], t["g_post_mix_2"].partition_broadcast(P)).then_inc(row_a_in, 16)
            root(3, D)

            def rotate_in(s):
                pool.wait_ge(bu_read, s + 1)
                a, b = ssm_a[:, s % 3, :], ssm_b[:, s % 3, :]
                nc.gpsimd.tensor_tensor(a[:, 0:256], a[:, 0:256], b[:, 256:512], ALU.add)
                nc.gpsimd.tensor_tensor(a[:, 256:512], a[:, 256:512], b[:, 0:256], ALU.subtract).then_inc(v_ready, 1)

            def rotate_out(s):
                pool.wait_ge(scan_done, s + 1)
                a = ssm_a[:, s % 3, :].rearrange("p (c t) -> p c t", c=2)
                b = ssm_b[:, s % 3, :].rearrange("p (c t) -> p c t", c=2)
                then(nc.gpsimd.tensor_tensor(a, b, cos_t[:, s, :].unsqueeze(1).to_broadcast([P, 2, S]), ALU.mult))
                nc.gpsimd.tensor_tensor(b, b, sin_t[:, s, :].unsqueeze(1).to_broadcast([P, 2, S]), ALU.mult).then_inc(prod_ready, 1)

            for s in range(ST + 1):
                if s == 6:
                    pool.wait_ge(rope_ready, 1)
                    for b in range(NB):
                        nc.gpsimd.tensor_copy(k_twice[:, b], qkv[:, b, SINK_H:SINK_H + KV_H, :].unsqueeze(2).to_broadcast([P, KV_H, 2, HD])).then_inc(k_twice_ready, 1)
                if s < ST:
                    rotate_in(s)
                if s >= 1:
                    rotate_out(s - 1)
            root(4, 512)
            root(5, 512)
            chunk_drained(pool, ("glu", 0))
            chunk_drained(pool, ("glu", 1))
            pool.dma_start(row_b[:], t["g_post_ffn_2"].partition_broadcast(P)).then_inc(row_b_in, 16)
            root(6, D)
            root(7, D)
            root(8, D)

        @block.scalar
        def _(act):
            next_unit = [0]

            def split_hi(until):
                for u in range(next_unit[0], min(until, n_units)):
                    act.wait_ge(landed[u % RING], 16 * (u // RING + 1))
                    if u >= RING:
                        act.wait_ge(unit_used, u - RING + 1)
                    nc.scalar.activation(w_hi[:, u % RING, :], stage[:, u % RING, :], ACT.Copy).then_inc(hi_ready, 1)
                next_unit[0] = max(next_unit[0], min(until, n_units))

            def ahead(name):
                split_hi(last_unit[name] + 1 + AHEAD)

            n_step = [0]

            def then(ins):
                n_step[0] += 1
                ins.then_inc(act_step, 1)
                act.wait_ge(act_step, n_step[0])

            act.dma_start(x[:], t["x"].rearrange("(b p) d -> p b d", p=P)).then_inc(x_in, 16)
            act.dma_start(ident[:], t["ident"]).then_inc(rows_in, 16)
            at = 0
            for name, n in (("even_norm", KD), ("odd_norm", KD), ("g_pre_mix_2", KD), ("g_pre_ffn_2", KD), ("g_ssm_out_2", CT),
                            ("g_attn_out_2", CT), ("ssm_d_2", CT), ("ssm_lambda_re_2", ST), ("ssm_lambda_im_2", ST)):
                act.dma_start(rows[at:at + n, :], t[name].rearrange("(n q) -> n q", q=P)).then_inc(rows_in, 16)
                at += n

            def squares(i, src, junk):
                for b in range(NB):
                    nc.scalar.activation(junk(b), src(b), ACT.Square, accum_out=sumsq[:, 2 * i + b:2 * i + b + 1]).then_inc(squared, 1)

            def hi_of_turned(first, tiles, at, gain):
                for k in range(tiles):
                    act.wait_ge(turned, first + (k | 1) + 1)
                    nc.scalar.activation(act_t[:, at + k, :], ps[:, 4 * BANK + ((at + k) % 8) * S:4 * BANK + ((at + k) % 8 + 1) * S], ACT.Copy,
                                         scale=col[:, gain + k:gain + k + 1]).then_inc(act_hi, 1)

            def hi_of_wide(first):
                for i in range(8):
                    act.wait_ge(turned, first + i + 1)
                    nc.scalar.activation(act_t[:, 2 * i:2 * i + 2, :], bank(4 + i % 4).rearrange("p (k n) -> p k n", k=2), ACT.Copy).then_inc(act_hi, 1)

            act.wait_ge(x_in, 16)
            squares(0, lambda b: x[:, b, :], lambda b: xs[:, b, :])
            split_hi(1)
            act.wait_ge(col_ready, 1)
            hi_of_turned(0, KD, 0, COL_EVEN)
            split_hi(4)
            act.wait_ge(ldt_ready, 1)
            nc.scalar.activation(sp["dt"][:], sp["ldt"][:], ACT.Exp).then_inc(dt_ready, 1)
            act.wait_ge(mdt_ready, 1)
            nc.scalar.activation(sp["mag"][:], sp["mdt"][:], ACT.Exp).then_inc(mag_ready, 1)
            act.wait_ge(ang_ready, 1)
            nc.scalar.activation(sm["sin"][:], sm["r"][:], ACT.Sin)
            nc.scalar.activation(sm["cos"][:], sm["abs"][:], ACT.Sin, bias=half_pi[:], scale=-1.0).then_inc(trig_ready, 1)
            act.wait_ge(params_in, 16 * 10)
            nc.scalar.activation(wf_hi[:], wf[:], ACT.Copy).then_inc(wf_hi_ready, 1)
            for half, kind in enumerate(("ga", "gb")):
                for c in range(2):
                    ahead((kind, c))
                    chunk_done(act, (kind, c))
                    nc.scalar.activation(gate0[half][:, :, c * 512:(c + 1) * 512], result((kind, c)), ACT.Silu).then_inc(drain_sem((kind, c)), 1)
            act.wait_ge(f_abs, 1)
            nc.scalar.activation(gate_f[:, 2], gate_f[:, 1], ACT.Exp).then_inc(f_exp, 1)
            act.wait_ge(f_exp, 1)
            nc.scalar.activation(gate_f[:, 3], gate_f[:, 2], ACT.Ln, bias=1.0).then_inc(f_ln, 1)

            def exponentials(n):
                act.wait_ge(scored, n + 1)
                e = prob[:, n % 3, :]
                nc.scalar.activation(e[:, 0:256], e[:, 0:256], ACT.Exp, bias=neg_max[:, 1, n:n + 1], scale=-1.0, accum_out=den[:, 1, n:n + 1])
                nc.scalar.activation(e[:, 256:384], e[:, 256:384], ACT.Exp, bias=neg_max[:, 0, n:n + 1], scale=-1.0,
                                     accum_out=den[:, 0, n:n + 1]).then_inc(exped, 1)

            for half in range(2):
                q, k, v = ("qa", "ka", "va") if half == 0 else ("qb", "kb", "vb")
                for c in range(2):
                    ahead((q, c))
                    chunk_done(act, (q, c))
                    nc.scalar.activation(q0[:, 4 * c:4 * c + 4, :].rearrange("p (a m) n -> p a (m n)", a=2), result((q, c)), ACT.Copy,
                                         scale=-(HD**-0.5)).then_inc(drain_sem((q, c)), 1)
                ahead((v, 1))
                for n in range(16 * half, 16 * half + 16):
                    exponentials(n)
            hi_of_wide(KD)
            for c in range(2):
                ahead(("even_out", c))
            chunk_drained(act, ("even_out", 0))
            chunk_drained(act, ("even_out", 1))
            squares(1, lambda b: x[:, b, :], lambda b: xs[:, b, :])
            hi_of_turned(KD + 8, KD, 0, COL_ODD)
            for kind, n in (("rq", 2), ("rk", 2), ("rv", 4)):
                for c in range(n):
                    ahead((kind, c))
            for c in range(4):
                ahead(("rg", c))
                chunk_done(act, ("rg", c))
                nc.scalar.activation(gate1[:, :, c * 512:(c + 1) * 512], result(("rg", c)), ACT.Silu).then_inc(drain_sem(("rg", c)), 1)
                act.wait_ge(wave_ready, 2 * c + 2)
                w = slice(4 * c, 4 * c + 4)
                then(nc.scalar.activation(cos_t[:, w, :], sin_t[:, w, :], ACT.Abs))
                nc.scalar.activation(sin_t[:, w, :], sin_t[:, w, :], ACT.Sin)
                nc.scalar.activation(cos_t[:, w, :], cos_t[:, w, :], ACT.Sin, bias=half_pi[:], scale=-1.0).then_inc(wave_sin, 1)
            for h in range(RET_H):
                act.wait_ge(ret_scale, h + 1)
                act.wait_ge(ret_gated, h + 1)
                for b in range(NB):
                    o = gate1[:, b, h * RET_V:(h + 1) * RET_V]
                    ins = nc.scalar.activation(o, o, ACT.Copy, scale=ret_rstd[:, h, b:b + 1])
                ins.then_inc(ret_out, 1)
            hi_of_wide(2 * KD + 8)
            for c in range(2):
                ahead(("odd_out", c))
            chunk_drained(act, ("odd_out", 0))
            chunk_drained(act, ("odd_out", 1))
            squares(2, lambda b: x[:, b, :], lambda b: xs[:, b, :])
            act.wait_ge(h_ready, 2)
            squares(3, lambda b: x[:, b, :], lambda b: xs[:, b, :])
            hi_of_turned(2 * KD + 16, KD, 0, COL_MIX)
            ahead(("u", 0))
            chunk_done(act, ("u", 0))
            nc.scalar.activation(u_t[:].rearrange("p (a m) n -> p a (m n)", a=2), result(("u", 0)), ACT.Copy).then_inc(drain_sem(("u", 0)), 1)
            ahead(("sq", 0))
            chunk_done(act, ("sq", 0))
            nc.scalar.activation(qkv[:, :, 0:SINK_H, :], result(("sq", 0)).rearrange("p b (h d) -> p b h d", d=HD), ACT.Copy,
                                 scale=-(HD**-0.5)).then_inc(drain_sem(("sq", 0)), 1)
            ahead(("skv", 0))
            chunk_done(act, ("skv", 0))
            nc.scalar.activation(qkv[:, :, SINK_H:12, :], result(("skv", 0), 256).rearrange("p b (h d) -> p b h d", d=HD), ACT.Copy).then_inc(drain_sem(("skv", 0)), 1)
            act.wait_ge(qk_turned, 1)
            nc.scalar.activation(q_t[:].rearrange("p (a m) n -> p a (m n)", a=2), ps[:, 4 * BANK:6 * BANK].rearrange("p (a n) -> p a n", a=2), ACT.Copy)
            act.wait_ge(qk_turned, 2)
            nc.scalar.activation(k_t[:], bank(3).rearrange("p (k n) -> p k n", k=2), ACT.Copy).then_inc(qk_ready, 1)
            for n in range(32, 40):
                exponentials(n)
            act.wait_ge(sink_sum, 1)
            nc.scalar.activation(sink_exp[:], sink_exp[:], ACT.Exp).then_inc(sink_exped, 1)
            act.wait_ge(y_attn_ready, 1)
            squares(4, lambda b: y_attn[:, b, :], lambda b: q_t[:, 2 * b:2 * b + 2, :].rearrange("p k n -> p (k n)"))
            hi_of_turned(3 * KD + 16, 4, 4, COL_GATTN)
            for ct in range(CT):
                act.wait_ge(y_added, ct + 1)
                nc.scalar.activation(gelu_hi[:, ct, :], y_ssm[:, ct, :], ACT.Gelu_apprx_tanh).then_inc(gelu_hi_ready, 1)
                nc.scalar.activation(y_ssm[:, ct, :], y_ssm[:, ct, :], ACT.Gelu_apprx_tanh).then_inc(gelu_ready, 1)
            for c in range(2):
                ahead(("glu", c))
            chunk_drained(act, ("glu", 1))
            nc.scalar.activation(gate_z[:], gate_z[:], ACT.Sigmoid).then_inc(sig_ready, 1)
            act.wait_ge(ssm_out_ready, 1)
            squares(5, lambda b: ssm_out[:, b, :], lambda b: gate_z[:, b, :])
            hi_of_turned(3 * KD + 20, 4, 0, COL_GSSM)
            for c in range(2):
                ahead(("mix_out", c))
                chunk_done(act, ("mix_out", c))
                nc.scalar.activation(mixed[:, :, c * 512:(c + 1) * 512], result(("mix_out", c)), ACT.Copy).then_inc(drain_sem(("mix_out", c)), 1)
            chunk_drained(act, ("mix_out", 0))
            chunk_drained(act, ("mix_out", 1))
            squares(6, lambda b: mixed[:, b, :], lambda b: xs[:, b, :])
            act.wait_ge(x_ready, 2)
            squares(7, lambda b: x[:, b, :], lambda b: xs[:, b, :])
            hi_of_turned(3 * KD + 24, KD, 0, COL_FFN)

            def ff_hi_of(c):
                act.wait_ge(ff_ready, c + 1)
                nc.scalar.activation(ff_hi[:, 2 * c:2 * c + 2, :], ff_val[0].rearrange("p (k n) -> p k n", k=2), ACT.Copy).then_inc(ff_hi_ready, 1)

            for c in range(11):
                ahead(("ffn", c))
                chunk_done(act, ("ffn", c))
                if c >= 2:
                    act.wait_ge(ff_ready, c - 1)
                nc.scalar.activation(ff_tmp[c % 2], result(("ffn", c))[:, 0, :], ACT.Silu).then_inc(silu_ready, 1)
                ff_hi_of(c)
            for c in range(2):
                ahead(("down", c))
                chunk_done(act, ("down", c))
                nc.scalar.activation(down_out[:, :, c * 512:(c + 1) * 512], result(("down", c)), ACT.Copy).then_inc(drain_sem(("down", c)), 1)
            chunk_drained(act, ("down", 0))
            chunk_drained(act, ("down", 1))
            squares(8, lambda b: down_out[:, b, :], lambda b: down_junk[:, b, :])

        @block.vector
        def _(dve):
            next_unit = [0]

            def split_lo(until):
                for u in range(next_unit[0], min(until, n_units)):
                    dve.wait_ge(hi_ready, u + 1)
                    nc.vector.tensor_tensor(w_lo[:, u % RING, :], stage[:, u % RING, :], w_hi[:, u % RING, :].bitcast(F32), ALU.subtract).then_inc(lo_ready, 1)
                next_unit[0] = max(next_unit[0], min(until, n_units))

            def ahead(name):
                split_lo(last_unit[name] + 1 + AHEAD)

            n_step = [0]

            def then(ins):
                n_step[0] += 1
                ins.then_inc(dve_step, 1)
                dve.wait_ge(dve_step, n_step[0])

            TT, TS, STT = nc.vector.tensor_tensor, nc.vector.tensor_scalar, nc.vector.scalar_tensor_tensor

            def scale_rows(i, src, dst):
                dve.wait_ge(rstd_ready, i + 1)
                for b in range(NB):
                    TS(dst(b), src(b), rstd[:, 2 * i + b:2 * i + b + 1], None, ALU.mult).then_inc(xs_ready, 1)

            def lo_of_turned(n_hi, tiles, at, gain, lo_at):
                for k in range(tiles):
                    dve.wait_ge(act_hi, n_hi + (k | 1) + 1)
                    src = ps[:, 4 * BANK + ((at + k) % 8) * S:4 * BANK + ((at + k) % 8 + 1) * S]
                    STT(act_t[:, lo_at + k, :], src, col[:, gain + k:gain + k + 1], act_t[:, at + k, :].bitcast(F32), ALU.mult, ALU.subtract).then_inc(act_lo, 1)

            def lo_of_wide(n_hi):
                for i in range(8):
                    dve.wait_ge(act_hi, n_hi + i + 1)
                    TT(y_lo[:, 2 * i:2 * i + 2, :], bank(4 + i % 4).rearrange("p (k n) -> p k n", k=2), act_t[:, 2 * i:2 * i + 2, :].bitcast(F32), ALU.subtract).then_inc(act_lo, 1)

            nc.vector.memset(half_pi[:], PI / 2)
            nc.vector.memset(neg_half[:], -0.5).then_inc(fills, 1)
            dve.wait_ge(col_turned, 1)
            nc.vector.tensor_copy(col[:], ps[:, 0:N_ROWS]).then_inc(col_ready, 1)
            scale_rows(0, lambda b: x[:, b, :], lambda b: xs[:, b, :])
            split_lo(1)
            dve.wait_ge(col_ready, 1)
            lo_of_turned(0, KD, 0, COL_EVEN, KD)
            split_lo(4)
            dve.wait_ge(params_in, 16 * 10)
            dve.wait_ge(tables_in, 16 * 7)
            for a in range(2):
                r = slice(a * SSM_N, (a + 1) * SSM_N)
                ins = nc.vector.tensor_copy(sp["ldt"][r, :], log_dt[r, :].rearrange("p (t a) -> p t a", a=2)[:, :, a])
            ins.then_inc(ldt_ready, 1)
            TS(sp["lre"][:], col[:, COL_LRE:COL_LRE + ST], -1e-4, None, ALU.min)
            TS(neg_sink[:], sink[:], -1.0, None, ALU.mult)
            then(nc.vector.tensor_copy(pos[:], pos_i[:]))
            for b in range(NB):
                TS(sm["ang"][:, ST + b * ROPE_HALF:ST + (b + 1) * ROPE_HALF], inv_freq[:], pos[:, b:b + 1], None, ALU.mult)
            dve.wait_ge(dt_ready, 1)
            TT(sp["mdt"][:], sp["lre"][:], sp["dt"][:], ALU.mult).then_inc(mdt_ready, 1)
            then(TT(sm["ang"][:, 0:ST], col[:, COL_LIM:COL_LIM + ST], sp["dt"][:], ALU.mult))

            def reduce_angle(ang, k, r):
                then(TS(k, ang, INV_2PI, ROUND_INT, ALU.mult, ALU.add))
                then(TS(k, k, -ROUND_INT, None, ALU.add))
                then(STT(r, k, -TWO_PI_1, ang, ALU.mult, ALU.add))
                then(STT(r, k, -TWO_PI_2, r, ALU.mult, ALU.add))
                then(STT(r, k, -TWO_PI_3, r, ALU.mult, ALU.add))

            reduce_angle(sm["ang"][:], sm["k"][:], sm["r"][:])
            then(TS(sm["r"][:], sm["r"][:], PI, -PI, ALU.min, ALU.max))
            STT(sm["abs"][:], sm["r"][:], -1.0, sm["r"][:], ALU.mult, ALU.max).then_inc(ang_ready, 1)
            then(TS(sp["hi"][:], sm["r"][:, 0:ST], ROUND_13, None, ALU.add))
            then(TS(sp["hi"][:], sp["hi"][:], -ROUND_13, None, ALU.add))
            then(TT(sp["lo"][:], sm["r"][:, 0:ST], sp["hi"][:], ALU.subtract))
            split_lo(last_unit[("ga", 0)] + 1)
            dve.wait_ge(mag_ready, 1)
            dve.wait_ge(trig_ready, 1)
            lre, lim = sp["lre"][:], col[:, COL_LIM:COL_LIM + ST]
            then(TT(sp["ar"][:], sp["mag"][:], sm["cos"][:, 0:ST], ALU.mult))
            then(TS(sp["ar"][:], sp["ar"][:], -1.0, None, ALU.add))
            then(TT(sp["ai"][:], sp["mag"][:], sm["sin"][:, 0:ST], ALU.mult))
            then(TT(sp["den"][:], lre, lre, ALU.mult))
            then(TT(sp["t"][:], lim, lim, ALU.mult))
            then(TT(sp["den"][:], sp["den"][:], sp["t"][:], ALU.add))
            then(nc.vector.reciprocal(sp["den"][:], sp["den"][:]))
            then(TT(sp["fr"][:], sp["ar"][:], lre, ALU.mult))
            then(TT(sp["t"][:], sp["ai"][:], lim, ALU.mult))
            then(TT(sp["fr"][:], sp["fr"][:], sp["t"][:], ALU.add))
            then(TT(sp["fr"][:], sp["fr"][:], sp["den"][:], ALU.mult))
            then(TT(sp["fi"][:], sp["ai"][:], lre, ALU.mult))
            then(TT(sp["t"][:], sp["ar"][:], lim, ALU.mult))
            then(TT(sp["fi"][:], sp["fi"][:], sp["t"][:], ALU.subtract))
            then(TT(sp["fi"][:], sp["fi"][:], sp["den"][:], ALU.mult))
            ahead(("ga", 0))
            dve.wait_ge(wf_hi_ready, 1)
            TT(wf_lo[:], wf[:], wf_hi[:].bitcast(F32), ALU.subtract).then_inc(wf_lo_ready, 1)
            fr_b = sp["fr"][:].unsqueeze(2).to_broadcast([P, ST, SSM_C])
            fi_b = sp["fi"][:].unsqueeze(2).to_broadcast([P, ST, SSM_C])
            dve.wait_ge(b_wide_ready, 1)
            for i, (f0, f1, op) in enumerate(((fr_b, fi_b, ALU.subtract), (fi_b, fr_b, ALU.add))):
                TT(b_tmp[0][:], b_in[0][:], f0, ALU.mult)
                then(TT(b_tmp[1][:], b_in[1][:], f1, ALU.mult))
                for a in range(2):
                    r = slice(a * SSM_N, (a + 1) * SSM_N)
                    ins = TT(b_wide[i][r, :, a, :], b_tmp[0][r], b_tmp[1][r], op)
                if i == 0:
                    then(ins)
            ins.then_inc(b_wide_ready, 1)
            for c in range(1, 4):
                ahead((("ga", "ga", "gb", "gb")[c], c % 2))
            dve.wait_ge(f_done, 1)
            f_in, f_neg = gate_f[:, 0], gate_f[:, 1]
            for b in range(NB):
                ins = TT(gate_f[:, 0, b, :], bank(4, FOX_H, b * FOX_H), bf[:], ALU.add)
            then(ins)
            STT(f_neg, f_in, -1.0, f_in, ALU.mult, ALU.min).then_inc(f_abs, 1)
            then(TS(f_in, f_in, 0.0, None, ALU.min))
            dve.wait_ge(f_ln, 1)
            TT(f_in, f_in, gate_f[:, 3], ALU.subtract).then_inc(f_ready, 1)
            ahead(("qa", 0))
            dve.wait_ge(cum_done, 1)
            nc.vector.tensor_copy(cum_t[:], ps[0:FOX_H, 5 * BANK:5 * BANK + S]).then_inc(cum_ready, 1)
            ahead(("qa", 1))
            dve.wait_ge(b_turned, 1)
            nc.vector.tensor_copy(b_re[:].rearrange("p t n -> p (t n)"), bank(6))
            nc.vector.tensor_copy(b_im[:].rearrange("p t n -> p (t n)"), bank(7)).then_inc(b_ready, 1)
            dve.wait_ge(c_turned, 1)
            nc.vector.tensor_copy(c_re[:].rearrange("p t n -> p (t n)"), bank(4))
            TS(c_re_neg[:].rearrange("p t n -> p (t n)"), bank(4), -1.0, None, ALU.mult)
            TS(c_im_neg[:].rearrange("p t n -> p (t n)"), bank(5), -1.0, None, ALU.mult).then_inc(c_ready, 1)

            def score_max(n, table):
                dve.wait_ge(scores, n + 1)
                src, dst = bank(n % 2), prob[:, n % 3, :]
                big = 3e38
                ttr = nc.vector.tensor_tensor_reduce
                if table == 0:
                    dve.wait_ge(forget_bias_ready, n // 4 + 1)
                    bias1, bias0 = forget_bias[:, n, :], forget_bias0[:, n, :]
                else:
                    bias1, bias0 = neg_bias[:, table, :], neg_bias[:, table, P:S]
                ttr(dst[:, 0:256], src[:, 0:256], bias1, 1.0, big, ALU.add, ALU.min, neg_max[:, 1, n:n + 1])
                ins = ttr(dst[:, 256:384], src[:, 256:384], bias0, 1.0, big, ALU.add, ALU.min, neg_max[:, 0, n:n + 1])
                if table == 2:
                    h = n - 32
                    then(ins)
                    m = neg_max[:, :, n:n + 1]
                    ins = TT(m, m, neg_sink[:, h:h + 1].unsqueeze(1).to_broadcast([P, NB, 1]), ALU.min)
                ins.then_inc(scored, 1)

            def copy_prob(n):
                dve.wait_ge(prob_turned, n + 1)
                if n >= 2:
                    dve.wait_ge(pv_done, n - 1)
                nc.vector.tensor_copy(prob_t[:, n % 2, :], bank(2 + n % 2, 384)).then_inc(prob_copied, 1)

            def invert(g):
                dve.wait_ge(exped, 8 * g + 8)
                nc.vector.reciprocal(inv_den[:, :, 8 * g:8 * g + 8], den[:, :, 8 * g:8 * g + 8]).then_inc(inv_ready, 1)

            def gate_heads(g):
                dve.wait_ge(pv_done, 8 * g + 8)
                dve.wait_ge(gate_scaled, g + 1)
                o = ps[:, (4 + 2 * (g % 2)) * BANK:(6 + 2 * (g % 2)) * BANK].rearrange("p (b n) -> p b n", b=2)
                dst = gate0[g // 2][:, :, (g % 2) * 512:(g % 2) * 512 + 512]
                TT(dst, o, dst, ALU.mult).then_inc(heads_out, 1)

            for half in range(2):
                names = ("ka", "va") if half == 0 else ("kb", "vb")
                if half == 1:
                    ahead(("qb", 0))
                    ahead(("qb", 1))
                for name in names:
                    for c in range(2):
                        ahead((name, c))
                        chunk_done(dve, (name, c))
                        src = result((name, c))
                        if name[0] == "k":
                            dst = k0[:, 4 * c:4 * c + 4, :].rearrange("p (a m) n -> p a (m n)", a=2)
                        else:
                            dst = v0[:, :, c * 512:(c + 1) * 512]
                        nc.vector.tensor_copy(dst, src).then_inc(drain_sem((name, c)), 1)
                for i in range(16 + 4):
                    n = 16 * half + i
                    if i < 16:
                        score_max(n, half)
                    if 2 <= i < 18:
                        copy_prob(n - 2)
                    if i % 8 == 1 and i >= 9:
                        invert((n - 9) // 8)
                    if i % 8 == 3 and i >= 11:
                        gate_heads((n - 11) // 8)

            def add_to_x(kind):
                for c in range(2):
                    ahead((kind, c))
                    chunk_done(dve, (kind, c))
                    dst = x[:, :, c * 512:(c + 1) * 512]
                    TT(dst, result((kind, c)), dst, ALU.add).then_inc(drain_sem((kind, c)), 1)

            lo_of_wide(KD)
            add_to_x("even_out")
            scale_rows(1, lambda b: x[:, b, :], lambda b: xs[:, b, :])
            lo_of_turned(KD + 8, KD, 0, COL_ODD, KD)

            for kind, dst in (("rq", q1), ("rk", k1)):
                for c in range(2):
                    ahead((kind, c))
                    chunk_done(dve, (kind, c))
                    for hh in range(2):
                        h = 2 * c + hh
                        src = result((kind, c))[:, hh, :].rearrange("p (e n) -> p e n", e=2)
                        by_cos = prob_t[:, :, :].rearrange("p a b -> p (a b)")[:, 0:512].rearrange("p (e n) -> p e n", e=2)
                        by_sin = prob[:, :, :].rearrange("p a b -> p (a b)")[:, 512:1024].rearrange("p (e n) -> p e n", e=2)
                        TT(by_cos, src, rot[:, 0, :].unsqueeze(1).to_broadcast([P, 2, S]), ALU.mult)
                        ins = TT(by_sin, src, rot[:, 1, :].unsqueeze(1).to_broadcast([P, 2, S]), ALU.mult)
                        then(ins)
                        TT(dst[:, h, 0, :], by_cos[:, 0, :], by_sin[:, 1, :], ALU.subtract)
                        ins = TT(dst[:, h, 1, :], by_sin[:, 0, :], by_cos[:, 1, :], ALU.add)
                        if hh == 0:
                            then(ins)
                    ins.then_inc(drain_sem((kind, c)), 1)
                    dve.wait_ge(drain_sem((kind, c)), number[(kind, c)] // 2 + 1)
            for c in range(4):
                ahead(("rv", c))
                chunk_done(dve, ("rv", c))
                nc.vector.tensor_copy(v1[:, :, c * 512:(c + 1) * 512], result(("rv", c))).then_inc(drain_sem(("rv", c)), 1)
            for c in range(4):
                ahead(("rg", c))
            for h in range(RET_H + 1):
                if h < RET_H:
                    dve.wait_ge(ret_scores, h + 1)
                    if h >= 2:
                        dve.wait_ge(ret_pv, h - 1)
                    s, d = bank(h % 2), prob_t[:, h % 2, :]
                    TT(d[:, 0:256], s[:, 0:256], decay[:, h, :], ALU.mult)
                    TT(d[:, 256:384], s[:, 256:384], decay[:, h, 0:P], ALU.mult).then_inc(ret_decayed, 1)
                if h >= 1:
                    g = h - 1
                    dve.wait_ge(ret_pv, g + 1)
                    for b in range(NB):
                        o = bank((2 if g % 2 == 0 else 4) + b)
                        then(nc.vector.bn_stats(stats[:, b, :], o))
                        ins = nc.vector.bn_aggr(mean_var[:, g, b, :], stats[:, b, :])
                        if b == 0:
                            then(ins)
                    ins.then_inc(ret_var, 1)
                    dve.wait_ge(ret_var, g + 1)
                    for b in range(NB):
                        o = bank((2 if g % 2 == 0 else 4) + b)
                        dst = gate1[:, b, g * RET_V:(g + 1) * RET_V]
                        ins = STT(dst, o, mean_var[:, g, b, 0:1], dst, ALU.subtract, ALU.mult)
                    ins.then_inc(ret_gated, 1)
            lo_of_wide(2 * KD + 8)
            add_to_x("odd_out")
            dve.wait_ge(rstd_ready, 3)
            dve.wait_ge(row_a_in, 16)
            for b in range(NB):
                ins = STT(x[:, b, :], x[:, b, :], rstd[:, 4 + b:5 + b], row_a[:], ALU.mult, ALU.mult)
                ins.then_inc(h_ready, 1)
            dve.wait_ge(h_ready, 2)
            scale_rows(3, lambda b: x[:, b, :], lambda b: xs[:, b, :])
            lo_of_turned(2 * KD + 16, KD, 0, COL_MIX, KD)
            ahead(("u", 0))

            def ssm(s):
                if s in (7, 11, 15):
                    add_skip((s - 7) // 4)
                if s < ST:
                    dve.wait_ge(bu_done, s + 1)
                    if s >= 3:
                        dve.wait_ge(y_done, s - 2)
                    if s % 4 == 0:
                        dve.wait_ge(wave_sin, s // 4 + 1)
                    src = bank(6).rearrange("p (c t) -> p c t", c=2)
                    a = ssm_a[:, s % 3, :].rearrange("p (c t) -> p c t", c=2)
                    b = ssm_b[:, s % 3, :].rearrange("p (c t) -> p c t", c=2)
                    TT(a, src, cos_t[:, s, :].unsqueeze(1).to_broadcast([P, 2, S]), ALU.mult)
                    TT(b, src, sin_t[:, s, :].unsqueeze(1).to_broadcast([P, 2, S]), ALU.mult).then_inc(bu_read, 1)
                if s >= 1:
                    r = s - 1
                    dve.wait_ge(v_ready, r + 1)
                    for c in range(2):
                        part = slice(c * S, (c + 1) * S)
                        ins = nc.vector.tensor_tensor_scan(ssm_b[:, r % 3, part], sp["mag"][:, r:r + 1].to_broadcast([P, S]), ssm_a[:, r % 3, part],
                                                           0.0, ALU.mult, ALU.add)
                    ins.then_inc(scan_done, 1)

            def add_skip(ct):
                dve.wait_ge(y_done, 4 * ct + 4)
                STT(y_ssm[:, ct, :], u_t[:, ct, :], col[:, COL_SKIP + ct:COL_SKIP + ct + 1], bank(7, S), ALU.mult, ALU.add).then_inc(y_added, 1)

            s_next = 0
            for u in range(4):
                ssm(s_next)
                s_next += 1
                split_lo(last_unit[("u", 0)] + 1 + AHEAD + 1 + u)
            for u in range(2):
                ssm(s_next)
                s_next += 1
                split_lo(last_unit[("sq", 0)] + 1 + AHEAD + 1 + u)
            chunk_drained(dve, ("sq", 0))
            chunk_drained(dve, ("skv", 0))
            NR = SINK_H + KV_H
            for b in range(NB):
                lo8, hi8 = qkv[:, b, 0:NR, 0:ROPE_HALF], qkv[:, b, 0:NR, ROPE_HALF:2 * ROPE_HALF]
                tmp = [rope_tmp[:, 0, i * 80:(i + 1) * 80].rearrange("p (h d) -> p h d", d=ROPE_HALF) for i in range(4)]
                at = ST + b * ROPE_HALF
                cosb = sm["cos"][:, at:at + ROPE_HALF].unsqueeze(1).to_broadcast([P, NR, ROPE_HALF])
                sinb = sm["sin"][:, at:at + ROPE_HALF].unsqueeze(1).to_broadcast([P, NR, ROPE_HALF])
                TT(tmp[0], lo8, cosb, ALU.mult)
                TT(tmp[1], hi8, sinb, ALU.mult)
                TT(tmp[2], hi8, cosb, ALU.mult)
                then(TT(tmp[3], lo8, sinb, ALU.mult))
                TT(lo8, tmp[0], tmp[1], ALU.subtract)
                ins = TT(hi8, tmp[2], tmp[3], ALU.add)
                if b == 0:
                    then(ins)
            ins.then_inc(rope_ready, 1)
            for i in range(8 + 3):
                if i < 8:
                    score_max(32 + i, 2)
                if 2 <= i < 10:
                    copy_prob(30 + i)
                if i == 8:
                    dve.wait_ge(scored, 40)
                    TT(sink_exp[:], neg_max[:, :, 32:40], sink[:].unsqueeze(1).to_broadcast([P, NB, SINK_H]), ALU.add).then_inc(sink_sum, 1)
                if s_next <= ST:
                    ssm(s_next)
                    s_next += 1
            dve.wait_ge(sink_exped, 1)
            dve.wait_ge(exped, 40)
            then(TT(den[:, :, 32:40], den[:, :, 32:40], sink_exp[:], ALU.add))
            then(nc.vector.reciprocal(inv_den[:, :, 32:40], den[:, :, 32:40]))
            dve.wait_ge(pv_done, 40)
            for b in range(NB):
                ins = TT(y_attn[:, b, :].rearrange("p (h d) -> p h d", d=HD), bank(4 + b).rearrange("p (h d) -> p h d", d=HD),
                         inv_den[:, b, 32:40].unsqueeze(2).to_broadcast([P, SINK_H, HD]), ALU.mult)
            ins.then_inc(y_attn_ready, 1)
            while s_next <= ST:
                ssm(s_next)
                s_next += 1
            add_skip(3)
            scale_rows(4, lambda b: y_attn[:, b, :], lambda b: y_attn[:, b, :])
            lo_of_turned(3 * KD + 16, 4, 4, COL_GATTN, KD + 4)
            for ct in range(CT):
                dve.wait_ge(gelu_ready, ct + 1)
                TT(gelu_lo[:, ct, :], y_ssm[:, ct, :], gelu_hi[:, ct, :].bitcast(F32), ALU.subtract).then_inc(gelu_lo_ready, 1)
            dve.wait_ge(row_b_in, 16)
            for c, dst in ((0, ssm_out), (1, gate_z)):
                ahead(("glu", c))
                chunk_done(dve, ("glu", c))
                for b in range(NB):
                    ins = TT(dst[:, b, :], result(("glu", c))[:, b, :], row_b[:, c * 512:(c + 1) * 512], ALU.add)
                    if b == 0:
                        continue
                    ins.then_inc(drain_sem(("glu", c)), 1)
            chunk_drained(dve, ("glu", 0))
            chunk_drained(dve, ("glu", 1))
            dve.wait_ge(sig_ready, 1)
            TT(ssm_out[:], ssm_out[:], gate_z[:], ALU.mult).then_inc(ssm_out_ready, 1)
            dve.wait_ge(ssm_out_ready, 1)
            scale_rows(5, lambda b: ssm_out[:, b, :], lambda b: ssm_out[:, b, :])
            lo_of_turned(3 * KD + 20, 4, 0, COL_GSSM, KD)
            for c in range(2):
                ahead(("mix_out", c))
            dve.wait_ge(rstd_ready, 7)
            dve.wait_ge(row_a_in, 32)
            for b in range(NB):
                then(STT(mixed[:, b, :], mixed[:, b, :], rstd[:, 12 + b:13 + b], row_a[:], ALU.mult, ALU.mult))
                TT(x[:, b, :], x[:, b, :], mixed[:, b, :], ALU.add).then_inc(x_ready, 1)
            dve.wait_ge(x_ready, 2)
            scale_rows(7, lambda b: x[:, b, :], lambda b: xs[:, b, :])
            lo_of_turned(3 * KD + 24, KD, 0, COL_FFN, KD)
            for c in range(11):
                ahead(("ffn", c))
                dve.wait_ge(silu_ready, c + 1)
                if c >= 1:
                    dve.wait_ge(ff_hi_ready, c)
                TT(ff_val[0], result(("ffn", c))[:, 1, :], ff_tmp[c % 2], ALU.mult).then_inc(ff_ready, 1)
                dve.wait_ge(ff_hi_ready, c + 1)
                TT(ff_lo[:, 2 * c:2 * c + 2, :], ff_val[0].rearrange("p (k n) -> p k n", k=2), ff_hi[:, 2 * c:2 * c + 2, :].bitcast(F32),
                   ALU.subtract).then_inc(drain_sem(("ffn", c)), 1)
            for c in range(2):
                ahead(("down", c))
            dve.wait_ge(rstd_ready, 9)
            dve.wait_ge(row_b_in, 32)
            for b in range(NB):
                then(STT(down_out[:, b, :], down_out[:, b, :], rstd[:, 16 + b:17 + b], row_b[:], ALU.mult, ALU.mult))
                TT(x[:, b, :], x[:, b, :], down_out[:, b, :], ALU.add).then_inc(h_ready, 1)

        @block.tensor
        def _(pe):
            mm = nc.tensor.matmul

            def turn_rows(src, kts, at, first_kt=0):
                for k in range(kts):
                    for b in range(NB):
                        o = 4 * BANK + ((at + k) % 8) * S + b * P
                        ins = nc.tensor.transpose(ps[:, o:o + P], src(b, first_kt + k), ident[:])
                    ins.then_inc(turned, 1)

            def turn_wide(src, lo_before):
                for i in range(8):
                    if i >= 4:
                        pe.wait_ge(act_lo, lo_before + i - 3)
                    for kk in range(2):
                        for b in range(NB):
                            o = (4 + i % 4) * BANK + kk * S + b * P
                            ins = nc.tensor.transpose(ps[:, o:o + P], src(b, 2 * i + kk), ident[:])
                    ins.then_inc(turned, 1)

            def start_chunk(name):
                n = number[name]
                if n >= 2:
                    pe.wait_ge(drained[n % 2], n // 2)

            def unit_of(name, j):
                u = chunks[name][0] + j
                pe.wait_ge(lo_ready, u + 1)
                per = chunks[name][2]
                view = lambda w: w[:, u % RING, :].rearrange("p (t n) -> p t n", t=per)
                return view(w_hi), view(w_lo)

            def tokens_unit(name, j, a_hi, a_lo, k_tiles, before=None):
                per = chunks[name][2]
                width = UNIT // per
                hi, lo = unit_of(name, j)
                out = result(name, width)
                for i in range(per):
                    k = j * per + i
                    if before is not None:
                        before(k)
                    for b in range(NB):
                        tok = slice(b * P, (b + 1) * P)
                        passes = ((a_hi(k)[:, tok], hi[:, i, :]), (a_hi(k)[:, tok], lo[:, i, :]), (a_lo(k)[:, tok], hi[:, i, :]))
                        for n, (left, right) in enumerate(passes):
                            ins = mm(out[:, b, :], left, right, start=(k == 0 and n == 0), stop=(k == k_tiles - 1 and n == 2))
                ins.then_inc(unit_used, 1)

            def channels_unit(name, j, k_tiles, columns, before=None):
                hi, lo = unit_of(name, j)
                out = result(name)
                for i in range(2):
                    k = 2 * j + i
                    if before is not None:
                        before(k)
                    for m in range(4):
                        o = out[:, m // 2, (m % 2) * S:(m % 2 + 1) * S]
                        passes = ((columns(hi[:, i, :], m), act_t[:, k, :]), (columns(lo[:, i, :], m), act_t[:, k, :]),
                                  (columns(hi[:, i, :], m), act_t[:, KD + k, :]))
                        for n, (left, right) in enumerate(passes):
                            ins = mm(o, left, right, start=(k == 0 and n == 0 and m % 2 == 0), stop=(k == k_tiles - 1 and n == 2), skip_group_check=True)
                ins.then_inc(unit_used, 1)

            def ffn_unit(name, j, before=None):
                hi, lo = unit_of(name, j)
                for i in range(4):
                    k = (j // 2) * 4 + i
                    if before is not None:
                        before(k)
                    for m in range(2):
                        o, w = result(name)[:, j % 2, m * S:(m + 1) * S], slice(m * P, (m + 1) * P)
                        passes = ((hi[:, i, w], act_t[:, k, :]), (lo[:, i, w], act_t[:, k, :]), (hi[:, i, w], act_t[:, KD + k, :]))
                        for n, (left, right) in enumerate(passes):
                            ins = mm(o, left, right, start=(k == 0 and n == 0 and m == 0), stop=(k == KD - 1 and n == 2), skip_group_check=True)
                ins.then_inc(unit_used, 1)

            x_hi = lambda k: act_t[:, k, :]
            x_lo = lambda k: act_t[:, KD + k, :]
            plain = lambda w, m: w[:, m * P:(m + 1) * P]

            def tokens(name, before=None):
                start_chunk(name)
                for j in range(chunks[name][1]):
                    tokens_unit(name, j, x_hi, x_lo, KD, before)

            def channels(name, columns=plain, before=None):
                start_chunk(name)
                for j in range(chunks[name][1]):
                    channels_unit(name, j, KD, columns, before)

            def after_lo(count):
                return lambda k: pe.wait_ge(act_lo, count + k + 1)

            pe.wait_ge(rows_in, 16 * 10)
            nc.tensor.transpose(ps[:, 0:N_ROWS], rows[0:N_ROWS, :], ident[0:N_ROWS, 0:N_ROWS]).then_inc(col_turned, 1)
            pe.wait_ge(xs_ready, 2)
            turn_rows(lambda b, k: xs[:, b, k * P:(k + 1) * P], KD, 0)
            pe.wait_ge(col_ready, 1)
            tokens(("ga", 0), after_lo(0))
            for name in (("ga", 1), ("gb", 0), ("gb", 1)):
                tokens(name)
            pe.wait_ge(wf_lo_ready, 1)
            for b in range(NB):
                tok = slice(b * P, (b + 1) * P)
                for k in range(KD):
                    passes = ((x_hi(k)[:, tok], wf_hi[:, k, :]), (x_hi(k)[:, tok], wf_lo[:, k, :]), (x_lo(k)[:, tok], wf_hi[:, k, :]))
                    for n, (left, right) in enumerate(passes):
                        ins = mm(bank(4, FOX_H, b * FOX_H), left, right, start=(k == 0 and n == 0), stop=(k == KD - 1 and n == 2))
            ins.then_inc(f_done, 1)
            channels(("qa", 0))
            pe.wait_ge(f_ready, 1)
            for b in range(NB):
                ins = mm(ps[0:FOX_H, 5 * BANK:5 * BANK + S], gate_f[:, 0, b, :], prefix[:, b, :], start=(b == 0), stop=(b == NB - 1))
            ins.then_inc(cum_done, 1)
            channels(("qa", 1))
            pe.wait_ge(b_wide_ready, 2)
            for i in range(2):
                for ct in range(CT):
                    src = b_wide[i][:, 4 * ct:4 * ct + 4, :, :].rearrange("p t a h -> p (t a h)")
                    ins = nc.tensor.transpose(bank(6 + i, P, ct * P), src, ident[:])
            ins.then_inc(b_turned, 1)
            pe.wait_ge(c_wide_ready, 4)
            pe.wait_ge(cum_ready, 1)
            for i in range(2):
                for ct in range(CT):
                    ins = nc.tensor.transpose(bank(4 + i, P, ct * P), c_wide[i][:, ct * P:(ct + 1) * P], ident[:])
            ins.then_inc(c_turned, 1)
            for name in (("ka", 0), ("ka", 1)):
                channels(name)
            for name in (("va", 0), ("va", 1)):
                tokens(name)

            def attend(first, heads, q_of, k_of, v_of, between=lambda i: None):
                for i in range(-2, heads + 1):
                    if i + 2 < heads:
                        n = first + i + 2
                        if n >= 2:
                            pe.wait_ge(scored, n - 1)
                        for at, width, tok in ((0, S, slice(P, S)), (2 * P, P, slice(0, P))):
                            o = bank(n % 2, width, at)
                            ins = mm(o, q_of(i + 2)[:, tok], k_of(i + 2)[:, 0:width], start=True, stop=True)
                        ins.then_inc(scores, 1)
                    if 0 <= i < heads:
                        n = first + i
                        pe.wait_ge(exped, n + 1)
                        if n >= 2:
                            pe.wait_ge(prob_copied, n - 1)
                        for part in range(3):
                            ins = nc.tensor.transpose(bank(2 + n % 2, P, part * P), prob[:, n % 3, part * P:(part + 1) * P], ident[:])
                        ins.then_inc(prob_turned, 1)
                    if i >= 1:
                        n = first + i - 1
                        g = n // 8
                        if n % 8 == 0 and 2 <= g < 4:
                            pe.wait_ge(heads_out, g - 1)
                        pe.wait_ge(prob_copied, n + 1)
                        e = prob_t[:, n % 2, :]
                        col_at = (n % 8) * HD
                        out = 4 + 2 * (g % 2)
                        mm(bank(out + 1, HD, col_at), e[:, 0:P], v_of(i - 1, 0), start=True, stop=False)
                        mm(bank(out + 1, HD, col_at), e[:, P:2 * P], v_of(i - 1, 1), start=False, stop=True)
                        mm(bank(out, HD, col_at), e[:, 2 * P:3 * P], v_of(i - 1, 0), start=True, stop=True).then_inc(pv_done, 1)
                    between(i)

            def layer0_attention(half):
                rows_of = lambda i: slice((i % 2) * HD, (i % 2 + 1) * HD)
                attend(16 * half, 16, lambda i: q0[rows_of(i), i // 2, :], lambda i: k0[rows_of(i), i // 2, :],
                       lambda i, b: v0[:, b, i * HD:(i + 1) * HD])

            pe.wait_ge(cum_ready, 1)
            pe.wait_ge(b_ready, 1)
            pe.wait_ge(c_ready, 1)
            pe.wait_ge(tables_in, 16 * 7)
            for name in (("ka", 0), ("ka", 1), ("va", 0), ("va", 1), ("qa", 0), ("qa", 1)):
                chunk_drained(pe, name)
            layer0_attention(0)
            for name in (("qb", 0), ("qb", 1), ("kb", 0), ("kb", 1)):
                channels(name)
            for name in (("vb", 0), ("vb", 1)):
                tokens(name)
            for name in (("vb", 0), ("vb", 1)):
                chunk_drained(pe, name)
            layer0_attention(1)

            def wide_out(kind, lo_before):
                for c in range(2):
                    name = (kind, c)
                    start_chunk(name)
                    for j in range(8):
                        tokens_unit(name, j, x_hi, lambda k: y_lo[:, k, :], 16, lambda k: pe.wait_ge(act_lo, lo_before + k // 2 + 1))

            pe.wait_ge(heads_out, 4)
            turn_wide(lambda b, k: gate0[k // 8][:, b, (k % 8) * P:(k % 8 + 1) * P], KD)
            wide_out("even_out", KD)
            pe.wait_ge(xs_ready, 4)
            turn_rows(lambda b, k: xs[:, b, k * P:(k + 1) * P], KD, 0)
            pairs = lambda w, m: w[:, (m // 2) * RET_QK:(m // 2 + 1) * RET_QK].rearrange("p (n e) -> p e n", e=2)[:, m % 2, :]
            channels(("rq", 0), pairs, after_lo(KD + 8))
            for name in (("rq", 1), ("rk", 0), ("rk", 1)):
                channels(name, pairs)
            for kind in ("rv", "rg"):
                for c in range(4):
                    tokens((kind, c))
            chunk_drained(pe, ("rg", 2))
            chunk_drained(pe, ("rg", 3))
            for h in range(RET_H + 1):
                if h < RET_H:
                    if h >= 2:
                        pe.wait_ge(ret_decayed, h - 1)
                    for kb, q_from, at in ((0, 0, 0), (1, P, 2 * P)):
                        for e in range(2):
                            ins = mm(bank(h % 2, S - q_from, at), k1[:, h, e, kb * P:(kb + 1) * P], q1[:, h, e, q_from:S], start=(e == 0), stop=(e == 1))
                    ins.then_inc(ret_scores, 1)
                if h >= 1:
                    g = h - 1
                    pe.wait_ge(ret_decayed, g + 1)
                    if g >= 2:
                        pe.wait_ge(ret_gated, g - 1)
                    o = 2 if g % 2 == 0 else 4
                    e, vv = prob_t[:, g % 2, :], slice(g * RET_V, (g + 1) * RET_V)
                    mm(bank(o), e[:, 0:P], v1[:, 0, vv], start=True, stop=True)
                    mm(bank(o + 1), e[:, P:2 * P], v1[:, 0, vv], start=True, stop=False)
                    mm(bank(o + 1), e[:, 2 * P:3 * P], v1[:, 1, vv], start=False, stop=True).then_inc(ret_pv, 1)
            pe.wait_ge(ret_out, RET_H)
            turn_wide(lambda b, k: gate1[:, b, k * P:(k + 1) * P], 2 * KD + 8)
            wide_out("odd_out", 2 * KD + 8)
            pe.wait_ge(xs_ready, 6)
            turn_rows(lambda b, k: xs[:, b, k * P:(k + 1) * P], KD, 0)
            channels(("u", 0), plain, after_lo(2 * KD + 16))

            def ssm(s):
                if s < ST:
                    if s >= 1:
                        pe.wait_ge(bu_read, s)
                    ct, r = s // 4, slice(32 * (s % 4), 32 * (s % 4) + 32)
                    mm(bank(6, S, 0), b_re[r, ct, :], u_t[r, ct, :], start=True, stop=True)
                    mm(bank(6, S, S), b_im[r, ct, :], u_t[r, ct, :], start=True, stop=True).then_inc(bu_done, 1)
                if s >= 3:
                    y = s - 3
                    ct, m = y // 4, slice(32 * (y % 4), 32 * (y % 4) + 32)
                    if y % 4 == 0 and ct >= 1:
                        pe.wait_ge(y_added, ct)
                    pe.wait_ge(prod_ready, y + 1)
                    a, b = ssm_a[:, y % 3, :], ssm_b[:, y % 3, :]
                    o = ps[m, 7 * BANK:7 * BANK + S]
                    products = ((c_re, a[:, 0:S]), (c_re_neg, b[:, S:2 * S]), (c_im_neg, b[:, 0:S]), (c_im_neg, a[:, S:2 * S]))
                    for n, (c, w) in enumerate(products):
                        ins = mm(o, c[:, ct, m], w, start=(n == 0), stop=(n == 3))
                    ins.then_inc(y_done, 1)

            chunk_drained(pe, ("u", 0))
            start_chunk(("sq", 0))
            for j in range(4):
                tokens_unit(("sq", 0), j, x_hi, x_lo, KD)
                ssm(j)
            start_chunk(("skv", 0))
            for j in range(2):
                tokens_unit(("skv", 0), j, x_hi, x_lo, KD)
                ssm(4 + j)
            pe.wait_ge(rope_ready, 1)
            for m in range(4):
                for b in range(NB):
                    ins = nc.tensor.transpose(ps[:, 4 * BANK + m * S + b * P:4 * BANK + m * S + (b + 1) * P], qkv[:, b, 2 * m:2 * m + 2, :].rearrange("p h d -> p (h d)"), ident[:])
            ins.then_inc(qk_turned, 1)
            pe.wait_ge(k_twice_ready, 2)
            for m in range(KV_H):
                for b in range(NB):
                    ins = nc.tensor.transpose(bank(3, P, m * S + b * P), k_twice[:, b, m].rearrange("p r d -> p (r d)"), ident[:])
            ins.then_inc(qk_turned, 1)
            pe.wait_ge(qk_ready, 1)
            rows_of = lambda i: slice((i % 2) * HD, (i % 2 + 1) * HD)
            attend(32, 8, lambda i: q_t[rows_of(i), i // 2, :], lambda i: k_t[rows_of(i), i // 4, :],
                   lambda i, b: qkv[:, b, SINK_H + KV_H + i // 4, :], lambda i: ssm(6 + i + 2))
            for s in range(6 + 11, ST + 3):
                ssm(s)
            pe.wait_ge(xs_ready, 8)
            turn_rows(lambda b, k: y_attn[:, b, k * P:(k + 1) * P], 4, 4)
            for c in range(2):
                name = ("glu", c)
                start_chunk(name)
                for j in range(2):
                    tokens_unit(name, j, lambda k: gelu_hi[:, k, :], lambda k: gelu_lo[:, k, :], CT,
                                lambda k: pe.wait_ge(gelu_lo_ready, k + 1))
            pe.wait_ge(xs_ready, 10)
            turn_rows(lambda b, k: ssm_out[:, b, k * P:(k + 1) * P], 4, 0)
            pe.wait_ge(act_lo, 3 * KD + 24)
            tokens(("mix_out", 0))
            tokens(("mix_out", 1))
            pe.wait_ge(xs_ready, 12)
            turn_rows(lambda b, k: xs[:, b, k * P:(k + 1) * P], KD, 0)
            for c in range(11):
                start_chunk(("ffn", c))
                for j in range(4):
                    ffn_unit(("ffn", c), j, after_lo(3 * KD + 24) if c == 0 else None)
            for n in (9, 10):
                chunk_drained(pe, ("ffn", n))
            for c in range(2):
                name = ("down", c)
                start_chunk(name)
                for j in range(KF // 2):
                    tokens_unit(name, j, lambda k: ff_hi[:, k, :], lambda k: ff_lo[:, k, :], KF)


_INPUTS = [
    "x", "even_norm", "even_w_in", "even_b_f", "even_w_out", "odd_norm", "odd_w_in", "odd_w_out", "final_norm",
    "positions_2", "g_pre_mix_2", "w_in_2", "ssm_lambda_re_2", "ssm_lambda_im_2", "ssm_log_dt_2", "ssm_b_re_2", "ssm_b_im_2",
    "ssm_c_re_2", "ssm_c_im_2", "ssm_d_2", "w_glu_2", "b_glu_2", "attn_sinks_2", "g_ssm_out_2", "g_attn_out_2", "w_out_2",
    "g_post_mix_2", "g_pre_ffn_2", "w_gate_up_2", "w_down_2", "g_post_ffn_2",
]
_MATRIX = {
    "x": (S, D), "even_w_in": (D, 8208), "even_w_out": (2048, D), "odd_w_in": (D, 6144), "odd_w_out": (2048, D),
    "w_in_2": (D, 1280), "w_glu_2": (512, 1024), "w_out_2": (D, D), "w_gate_up_2": (D, 2 * DFF), "w_down_2": (DFF, D),
    "ssm_b_re_2": (2048, 16), "ssm_b_im_2": (2048, 16), "ssm_c_re_2": (512, 64), "ssm_c_im_2": (512, 64),
}


def kernel(**inputs):
    import numpy as _np
    import concourse.bacc as _bacc
    from concourse import mybir as _mybir
    from concourse.bass_utils import run_bass_kernel_spmd as _run

    nc = _bacc.Bacc("TRN2", target_bir_lowering=False, num_devices=1)
    arrays, t = {}, {}
    given = {n: _np.ascontiguousarray(inputs[n]).reshape(_MATRIX.get(n, (-1,))) for n in _INPUTS}
    given.update(constant_tables())
    for name, a in given.items():
        arrays["in_" + name] = a
        t[name] = nc.dram_tensor("in_" + name, a.shape, _mybir.dt.from_np(a.dtype), kind="ExternalInput").ap()
    t["cum_forget"] = nc.dram_tensor("cum_forget", (FOX_H, S), _mybir.dt.float32, kind="Internal").ap()
    t["out"] = nc.dram_tensor("out_0", (S, D), _mybir.dt.float32, kind="ExternalOutput").ap()
    build(nc, t)
    r = _run(nc, [arrays], core_ids=[0])
    return r.results[0]["out_0"].reshape(1, S, D)
```

```python
from contextlib import ExitStack

import numpy as np

import concourse.bass as bass
from concourse import mybir

F32 = mybir.dt.float32
F32R = mybir.dt.float32r
I32 = mybir.dt.int32
ACT = mybir.ActivationFunctionType
ALU = mybir.AluOpType

P = 128
S = 256
NB = S // P
D = 1024
KD = D // P
HD = 64
FOX_H = DIL_H = 16
EVEN_W = 1024
RET_H, RET_QK, RET_V = 4, 256, 512
SSM_W, SSM_G, SSM_N, SSM_C = 512, 32, 64, 16
ST = SSM_G * SSM_N // P
CT = SSM_W // P
SINK_H, KV_H = 8, 2
DFF = 2816
KF = DFF // P
ROPE_HALF = 8
EPS = 1e-6
NEG = 1e30
BANK = 512

RING = 4
UNIT = 1024
SSM_BUFS = 4
SSM_EARLY = 6
SSM_STEPS = (2, 2) + 9 * (1,)
AHEAD = 3

PI = float(np.float32(np.pi))
TWO_PI_1 = 6.28125
TWO_PI_2 = float(np.float32(np.float32((2 * np.pi - TWO_PI_1) * 2**21).round() / 2**21))
TWO_PI_3 = float(np.float32(2 * np.pi - TWO_PI_1 - TWO_PI_2))
INV_2PI = float(np.float32(1 / (2 * np.pi)))
ROUND_INT = 1.5 * 2.0**23
ROUND_13 = 1.5 * 2.0**10


def constant_tables():
    q = np.arange(P)[:, None]
    far, near = P + q - np.arange(P)[None], q - np.arange(P)[None]
    dist = np.concatenate([far, near], 1)
    causal = np.where(dist >= 0, 0.0, NEG)
    times = ((dist >= 0) & (dist <= 128)).astype(int) + ((dist >= 0) & (dist % 4 == 0)) + ((dist >= 0) & (dist % 16 == 0))
    dilated = np.where(times > 0, -np.log(np.maximum(times, 1)), NEG)
    window = np.where((dist >= 0) & (dist < 128), 0.0, NEG)
    neg_bias = np.stack([causal, dilated, window], 1)
    half = RET_QK // 2
    inv = 1.0 / (np.float32(10000.0) ** np.linspace(0.0, 1.0, half, dtype=np.float32))
    ang = (np.arange(S, dtype=np.float32)[None] * inv.astype(np.float32)[:, None]).astype(np.float32)
    rot = np.stack([np.cos(ang), np.sin(ang)], 1)
    log_gamma = np.log1p(-(2.0 ** (-5.0 - np.arange(RET_H))))
    lag = np.arange(S)[None] - np.arange(P)[:, None]
    decay = np.where(lag[:, None] >= 0, np.exp(log_gamma[None, :, None] * np.maximum(lag, 0)[:, None]), 0.0) * RET_QK**-0.5
    inv_freq = np.float32(500000.0) ** (-np.arange(ROPE_HALF, dtype=np.float32) * np.float32(2.0 / 16))
    group_parity = (np.arange(P)[:, None] // SSM_C % 2 == np.arange(2)[None])
    steps = np.broadcast_to(np.arange(S)[None], (P, S))
    f = lambda a: np.ascontiguousarray(a, dtype=np.float32)
    return {
        "ident": f(np.eye(P)), "neg_bias": f(neg_bias), "rot": f(rot), "decay": f(decay),
        "inv_freq": f(np.broadcast_to(inv_freq[None], (P, ROPE_HALF))), "parity": f(group_parity), "steps": f(steps),
    }


def weight_chunks():
    table, unit = {}, 0

    def add(name, units, per_unit):
        nonlocal unit
        table[name] = (unit, units, per_unit, len(table))
        unit += units

    for name in ("ga", "gb", "qa", "ka", "va", "qb", "kb", "vb"):
        for c in range(2):
            add((name, c), KD // 2, 2)
    for c in range(2):
        add(("even_out", c), 2 * KD // 2, 2)
    for name, n in (("rq", 2), ("rk", 2), ("rv", 4), ("rg", 4)):
        for c in range(n):
            add((name, c), KD // 2, 2)
    for c in range(2):
        add(("odd_out", c), RET_H * RET_V // P // 2, 2)
    add(("u", 0), KD // 2, 2)
    add(("sq", 0), KD // 2, 2)
    add(("skv", 0), 2, 4)
    add(("mix_attn", 0), CT // 2, 2)
    for c in (1, 0):
        add(("glu", c), CT // 2, 2)
    add(("mix_attn", 1), CT // 2, 2)
    for c in range(2):
        add(("mix_ssm", c), CT // 2, 2)
    for c in range(DFF // 256):
        add(("ffn", c), 4, 4)
    for c in range(2):
        add(("down", c), KF // 2, 2)
    return table, unit


def build(nc, t):
    chunks, n_units = weight_chunks()
    number = {name: c[3] for name, c in chunks.items()}
    last_unit = {name: c[0] + c[1] - 1 for name, c in chunks.items()}

    with ExitStack() as ctx:
        sem = lambda name: ctx.enter_context(nc.semaphore(name))
        sb = lambda name, shape, dt=F32: ctx.enter_context(nc.sbuf_tensor(name, shape, dt))

        stage = sb("stage", [P, RING, UNIT])
        w_hi = sb("w_hi", [P, RING, UNIT], F32R)
        w_lo = sb("w_lo", [P, RING, UNIT], F32R)
        x = sb("x", [P, NB, D])
        act_t = sb("act_t", [P, 16, S], F32R)
        prob = sb("prob", [P, 3, 384])
        prob_t = sb("prob_t", [P, 2, 384])
        cos_t = sb("cos_t", [P, ST, S])
        sin_t = sb("sin_t", [P, ST, S])
        forget_bias = cos_t[:, 0:FOX_H, :]
        forget_bias0 = sin_t[:, :, :].rearrange("p a b -> p (a b)")[:, 0:FOX_H * P].rearrange("p (h k) -> p h k", h=FOX_H)
        mixed = sb("mixed", [P, NB, D])
        decay = mixed[:, 0, :].rearrange("p (h n) -> p h n", h=RET_H)
        wave_k, wave_part = (mixed[:, 1, i * 512:(i + 1) * 512].rearrange("p (s n) -> p s n", s=2) for i in range(2))
        b_re, b_im = sb("b_re", [P, CT, P]), sb("b_im", [P, CT, P])
        c_re, c_im_neg = sb("c_re", [P, CT, P]), sb("c_im_neg", [P, CT, P])
        row_a, row_b = sb("row_a", [P, D]), sb("row_b", [P, D])
        ident = sb("ident", [P, P])
        neg_bias = sb("neg_bias", [P, 3, S])
        rot = sb("rot", [P, 2, S])
        steps = sb("steps", [P, S])
        inv_freq, parity = sb("inv_freq", [P, ROPE_HALF]), sb("parity", [P, 2])
        N_ROWS = 5 * KD + 3 * CT + 2 * ST
        rows = sb("rows", [P, P])
        col = sb("col", [P, N_ROWS])
        COL_EVEN, COL_ODD, COL_MIX, COL_FFN = 0, KD, 2 * KD, 3 * KD
        COL_GSSM, COL_GATTN, COL_SKIP = 4 * KD, 4 * KD + CT, 4 * KD + 2 * CT
        COL_LRE = 4 * KD + 3 * CT
        COL_LIM = COL_LRE + ST
        COL_FINAL = COL_LIM + ST
        sumsq, sumsq_b, rstd = sb("sumsq", [P, 18]), sb("sumsq_b", [P, 18]), sb("rstd", [P, 18])
        rstd_in, rstd_in_q = sb("rstd_in", [P, NB]), sb("rstd_in_q", [P, NB])
        ones, diag = sb("ones", [P, P]), sb("diag", [P, NB, P])
        rstd_row, rstd_row_q = sb("rstd_row", [P, S]), sb("rstd_row_q", [P, S])
        neg_half, half_pi = sb("neg_half", [P, 8]), sb("half_pi", [P, 1])
        W_F = KD * FOX_H + P - FOX_H
        wf, wf_hi, wf_lo = sb("wf", [P, W_F]), sb("wf_hi", [P, W_F], F32R), sb("wf_lo", [P, W_F], F32R)
        bf = sb("bf", [FOX_H, 1])
        gate_f = sb("gate_f", [FOX_H, 4, S])
        cum_t = sb("cum_t", [FOX_H, S])
        N_HEADS = FOX_H + DIL_H + SINK_H
        neg_max, den, inv_den = sb("neg_max", [P, NB, N_HEADS]), sb("den", [P, NB, N_HEADS]), sb("inv_den", [P, NB, N_HEADS])
        sink, neg_sink, sink_exp = sb("sink", [P, SINK_H]), sb("neg_sink", [P, SINK_H]), sb("sink_exp", [P, NB, SINK_H])
        log_dt = sb("log_dt", [P, SSM_G])
        pos_i, pos = sb("pos_i", [P, NB], I32), sb("pos", [P, NB])
        NA = ST + NB * ROPE_HALF
        sm = {n: sb("sm_" + n, [P, NA]) for n in ("ang", "k", "r", "sin", "cos", "abs")}
        sp = {n: sb("sp_" + n, [P, ST]) for n in ("lre", "ldt", "dt", "mdt", "mag", "ar", "ai", "den", "t", "fr", "fi", "hi", "lo")}
        stats, mean_var, ret_rstd = sb("stats", [P, NB, 6]), sb("mean_var", [P, RET_H, NB, 2]), sb("ret_rstd", [P, RET_H, NB])

        WORK = 12288
        sb("work", [P, WORK])
        work_from = nc.sbuf_base - 4 * WORK

        def over(name, at, shape, dt=F32):
            return nc.alloc_sbuf_tensor_at(name, shape, dt, offset=work_from + 4 * at)

        junk = over("junk", 10240, [P, NB, D])
        q0, k0, v0 = over("q0", 0, [P, 8, S]), over("k0", 2048, [P, 8, S]), over("v0", 4096, [P, NB, 1024])
        gate0 = [over("gate_a", 6144, [P, NB, 1024]), over("gate_b", 8192, [P, NB, 1024])]
        b_in = [over("b_in_re", 10240, [P, ST, SSM_C]), over("b_in_im", 10496, [P, ST, SSM_C])]
        b_tmp = [over("b_tmp0", 10752, [P, ST, SSM_C]), over("b_tmp1", 11008, [P, ST, SSM_C])]
        b_wide = [over("b_wide_re", 11264, [P, ST, 2, SSM_C]), over("b_wide_im", 11776, [P, ST, 2, SSM_C])]
        c_in = [sb("c_in_re", [P, CT, SSM_N]), sb("c_in_im", [P, CT, SSM_N])]
        c_wide = [prob[:, :, :].rearrange("p a b -> p (a b)")[:, 0:512], prob[:, :, :].rearrange("p a b -> p (a b)")[:, 512:1024]]
        y_lo = over("y_lo", 0, [P, 16, S], F32R)
        q1, k1 = over("q1", 0, [P, RET_H, 2, S]), over("k1", 2048, [P, RET_H, 2, S])
        v1, gate1 = over("v1", 4096, [P, NB, 2048]), over("gate1", 8192, [P, NB, 2048])
        u_t = over("u_t", 0, [P, CT, S])
        qkv = over("qkv", 1024, [P, NB, 12, HD])
        k_twice = over("k_twice", 2560, [P, NB, KV_H, 2, HD])
        q_t, k_t = over("q_t", 3072, [P, 4, S]), over("k_t", 4096, [P, KV_H, S])
        y_attn = over("y_attn", 4608, [P, NB, 512])
        gelu_hi, gelu_lo = over("gelu_hi", 5632, [P, CT, S], F32R), over("gelu_lo", 6656, [P, CT, S], F32R)
        ssm_a, ssm_b = over("ssm_a", 8192, [P, SSM_BUFS, 512]), over("ssm_b", 10240, [P, SSM_BUFS, 512])
        y_ssm = [mixed[:, ct // 2, 512 + (ct % 2) * S:512 + (ct % 2 + 1) * S] for ct in range(CT)]
        ssm_out, gate_z = over("ssm_out", 1024, [P, NB, 512]), over("gate_z", 2048, [P, NB, 512])
        rope_tmp = over("rope_tmp", 7680, [P, 1, 512])
        ff_hi, ff_lo = over("ff_hi", 0, [P, KF, S], F32R), over("ff_lo", 5632, [P, KF, S], F32R)
        down_out, down_junk = (w[:, 0:8, :].rearrange("p (b k) n -> p b (k n)", b=NB) for w in (cos_t, sin_t))
        ff_raw = cos_t[:, 8:16, :].rearrange("p (i g m) n -> p i g (m n)", i=2, g=2)
        ff_val = sin_t[:, 8:12, :].rearrange("p (i m) n -> p i (m n)", i=2)

        ps = ctx.enter_context(nc.psum_tensor("ps", [P, 8 * BANK], F32))

        def bank(b, width=BANK, at=0):
            return ps[:, b * BANK + at:b * BANK + at + width]

        landed = [sem(f"unit_landed_{i}") for i in range(RING)]
        hi_ready, lo_ready, unit_used = sem("hi_ready"), sem("lo_ready"), sem("unit_used")
        drained = [sem("chunk_drained_even"), sem("chunk_drained_odd")]
        x_in, ident_in, rows_in, late_in, b_in_landed, tables_in, params_in = sem("x_in"), sem("ident_in"), sem("rows_in"), sem("late_in"), sem("b_in_landed"), sem("tables_in"), sem("params_in")
        row_a_in, row_b_in, out_stored = sem("row_a_in"), sem("row_b_in"), sem("out_stored")
        fills = sem("fills")
        squared, rstd_ready, rstd_in_ready = sem("squared"), sem("rstd_ready"), sem("rstd_in_ready")
        diag_ready, row_done, row_taken, mixed_ready = sem("diag_ready"), sem("row_done"), sem("row_taken"), sem("mixed_ready")
        down_scaled, down_scaled_b, down_copied = sem("down_scaled"), sem("down_scaled_b"), sem("down_copied")
        turned, act_hi, act_lo = sem("turned"), sem("act_hi"), sem("act_lo")
        x_ready, h_ready = sem("x_ready"), sem("h_ready")
        dve_step, act_step, pool_step = sem("dve_step"), sem("act_step"), sem("pool_step")
        col_turned, col_ready = sem("col_turned"), sem("col_ready")
        ldt_ready, dt_ready, mdt_ready, mag_ready = sem("ldt_ready"), sem("dt_ready"), sem("mdt_ready"), sem("mag_ready")
        ang_ready, trig_ready = sem("ang_ready"), sem("trig_ready")
        b_wide_ready, b_turned, b_ready = sem("b_wide_ready"), sem("b_turned"), sem("b_ready")
        c_wide_ready, c_turned, c_ready = sem("c_wide_ready"), sem("c_turned"), sem("c_ready")
        wf_hi_ready, wf_lo_ready, f_done, f_abs, f_exp, f_ln = (sem(n) for n in ("wf_hi_ready", "wf_lo_ready", "f_done", "f_abs", "f_exp", "f_ln"))
        cum_ready, v_block_ready = sem("cum_ready"), sem("v_block_ready")
        cum_stored, cum_spread, forget_bias_ready = sem("cum_stored"), sem("cum_spread"), sem("forget_bias_ready")
        scores, scored, exped, prob_turned, prob_copied, pv_done = (sem(n) for n in ("scores", "scored", "exped", "prob_turned", "prob_copied", "pv_done"))
        inv_ready, gate_scaled, heads_out = sem("inv_ready"), sem("gate_scaled"), sem("heads_out")
        wave_ready, wave_sin = sem("wave_ready"), sem("wave_sin")
        ret_scores, ret_decayed, ret_pv, ret_var, ret_scale, ret_gated, ret_out = (sem(n) for n in ("ret_scores", "ret_decayed", "ret_pv", "ret_var", "ret_scale", "ret_gated", "ret_out"))
        bu_done, bu_read, v_ready, scan_done, prod_ready, y_done, y_added = (sem(n) for n in ("bu_done", "bu_read", "v_ready", "scan_done", "prod_ready", "y_done", "y_added"))
        gelu_hi_ready, gelu_ready, gelu_lo_ready = sem("gelu_hi_ready"), sem("gelu_ready"), sem("gelu_lo_ready")
        rope_ready, k_twice_ready, qk_turned, qk_ready = sem("rope_ready"), sem("k_twice_ready"), sem("qk_turned"), sem("qk_ready")
        sink_sum, sink_exped, y_attn_ready = sem("sink_sum"), sem("sink_exped"), sem("y_attn_ready")
        sig_ready, ssm_out_ready = sem("sig_ready"), sem("ssm_out_ready")
        ff_raw_ready, silu_ready, ff_ready, ff_hi_ready, ff_lo_ready = sem("ff_raw_ready"), sem("silu_ready"), sem("ff_ready"), sem("ff_hi_ready"), sem("ff_lo_ready")

        def result(name, width=BANK):
            n = number[name]
            return ps[:, (n % 2) * 2 * BANK:(n % 2) * 2 * BANK + 2 * BANK].rearrange("p (b n) -> p b n", b=2)[:, :, 0:width]

        def chunk_done(eng, name):
            eng.wait_ge(unit_used, last_unit[name] + 1)

        def chunk_drained(eng, name):
            n = number[name]
            eng.wait_ge(drained[n % 2], n // 2 + 1)

        def drain_sem(name):
            return drained[number[name] % 2]

        EVEN_TURN_BANKS, ODD_TURN_BANKS = (4, 5, 2, 3, 6, 7, 4, 5), (6, 7, 2, 3, 4, 5, 6, 7)

        SPLIT = (1, 2, 6, 8)

        def squared_count(i):
            return sum(2 * NB if n in SPLIT else NB for n in range(i + 1))

        w_even = t["even_w_in"].rearrange("(t p) n -> p t n", p=P)
        even_at = {"qa": 0, "ka": 1024, "va": 2048, "ga": 3072, "fa": 4096, "qb": 4112, "kb": 5136, "vb": 6160, "gb": 7184}
        w_even_out = t["even_w_out"].rearrange("(t p) n -> p t n", p=P)
        w_odd = t["odd_w_in"].rearrange("(t p) n -> p t n", p=P)
        odd_at = {"rq": 0, "rk": 1024, "rv": 2048, "rg": 4096}
        w_odd_out = t["odd_w_out"].rearrange("(t p) n -> p t n", p=P)
        w_in = t["w_in_2"].rearrange("(t p) n -> p t n", p=P)
        in_at = {"u": 0, "sq": 512, "skv": 1024}
        w_glu = t["w_glu_2"].rearrange("(t p) n -> p t n", p=P)
        w_mix = t["w_out_2"].rearrange("(t p) n -> p t n", p=P)
        w_gu = t["w_gate_up_2"].rearrange("(t p) n -> p t n", p=P)
        w_down = t["w_down_2"].rearrange("(t p) n -> p t n", p=P)

        def unit_source(name, j):
            kind, c = name
            per = chunks[name][2]
            ks = slice(j * per, (j + 1) * per)
            if kind in even_at:
                return w_even[:, ks, even_at[kind] + c * 512:even_at[kind] + (c + 1) * 512]
            if kind in odd_at:
                return w_odd[:, ks, odd_at[kind] + c * 512:odd_at[kind] + (c + 1) * 512]
            if kind in in_at:
                return w_in[:, ks, in_at[kind]:in_at[kind] + UNIT // per]
            if kind == "ffn":
                at = (j % 2) * DFF + c * 256
                return w_gu[:, (j // 2) * 4:(j // 2 + 1) * 4, at:at + 256]
            if kind in ("mix_attn", "mix_ssm"):
                at = CT if kind == "mix_attn" else 0
                return w_mix[:, at + j * per:at + (j + 1) * per, c * 512:(c + 1) * 512]
            w = {"even_out": w_even_out, "odd_out": w_odd_out, "glu": w_glu, "down": w_down}[kind]
            return w[:, ks, c * 512:(c + 1) * 512]

        block = ctx.enter_context(nc.Block())

        @block.sync
        def _(sp_eng):
            sp_eng.dma_start(ident[:], t["ident"]).then_inc(ident_in, 16)
            sp_eng.dma_start(rows[0:N_ROWS, :], t["vectors"]).then_inc(rows_in, 16)
            for b in range(NB):
                sp_eng.dma_start(x[:, b, :], t["x"][b * P:(b + 1) * P, :]).then_inc(x_in, 16)
            for name, (first, units, per, _) in chunks.items():
                for j in range(units):
                    u = first + j
                    if u == RING:
                        for dst, src in ((neg_bias[:], t["neg_bias"]), (rot[:], t["rot"]), (steps[:], t["steps"]), (decay, t["decay"])):
                            sp_eng.dma_start(dst, src).then_inc(late_in, 16)
                    if u >= RING:
                        sp_eng.wait_ge(lo_ready, u - RING + 1)
                    dst = stage[:, u % RING, :].rearrange("p (t n) -> p t n", t=per)
                    sp_eng.dma_start(dst, unit_source(name, j)).then_inc(landed[u % RING], 16)
            for b in range(NB):
                for c in range(2):
                    half = slice(c * 512, (c + 1) * 512)
                    sp_eng.wait_ge(h_ready, NB + 2 * b + c + 1)
                    sp_eng.dma_start(t["out"][b * P:(b + 1) * P, half], x[:, b, half]).then_inc(out_stored, 16)
            sp_eng.wait_ge(out_stored, 16 * 2 * NB)

        @block.gpsimd
        def _(pool):
            n_step = [0]

            def then(ins):
                n_step[0] += 1
                ins.then_inc(pool_step, 1)
                pool.wait_ge(pool_step, n_step[0])

            for dst, src in ((inv_freq[:], t["inv_freq"]), (parity[:], t["parity"])):
                pool.dma_start(dst, src).then_inc(tables_in, 16)
            pool.dma_start(wf[:, 0:KD * FOX_H].rearrange("p (k h) -> p k h", k=KD), w_even[:, :, even_at["fa"]:even_at["fa"] + FOX_H]).then_inc(params_in, 16)
            pool.dma_start(bf[:], t["even_b_f"].rearrange("(h o) -> h o", o=1)).then_inc(params_in, 16)
            pool.dma_start(sink[:], t["attn_sinks_2"].partition_broadcast(P)).then_inc(params_in, 16)
            pool.dma_start(log_dt[:], t["ssm_log_dt_2"].partition_broadcast(P)).then_inc(params_in, 16)
            for b in range(NB):
                pool.dma_start(pos_i[:, b:b + 1], t["positions_2"].rearrange("(n o) -> n o", o=1)[b * P:(b + 1) * P, :]).then_inc(params_in, 16)
            for i, name in enumerate(("ssm_c_re_2", "ssm_c_im_2")):
                pool.dma_start(c_in[i][:], t[name].rearrange("(t q) n -> q t n", q=P)).then_inc(params_in, 16)

            def root(i, width):
                c = slice(2 * i, 2 * i + 2)
                pool.wait_ge(squared, squared_count(i))
                if i in SPLIT:
                    then(nc.gpsimd.tensor_tensor(sumsq[:, c], sumsq[:, c], sumsq_b[:, c], ALU.add))
                then(nc.gpsimd.tensor_scalar(rstd[:, c], sumsq[:, c], 1.0 / width, EPS, ALU.mult, ALU.add))
                nc.gpsimd.tensor_tensor(rstd[:, c], rstd[:, c], neg_half[:, 0:2], ALU.pow).then_inc(rstd_ready, 1)

            pool.wait_ge(fills, 1)
            root(0, D)
            for i, name in enumerate(("ssm_b_re_2", "ssm_b_im_2")):
                pool.dma_start(b_in[i][:], t[name].rearrange("(t q) h -> q t h", q=P)).then_inc(b_in_landed, 16)
            pool.dma_start(row_a[:], t["final_norm"].partition_broadcast(P)).then_inc(row_a_in, 16)
            pool.dma_start(row_b[:], t["b_glu_2"].partition_broadcast(P)).then_inc(row_b_in, 16)
            then(nc.gpsimd.memset(b_wide[0][:], 0.0))
            nc.gpsimd.memset(b_wide[1][:], 0.0).then_inc(b_wide_ready, 1)
            pool.wait_ge(params_in, 16 * 8)
            pool.wait_ge(tables_in, 16 * 2)
            for i in range(2):
                for a in range(2):
                    dst = c_wide[i].rearrange("p (t a n) -> p t a n", t=CT, a=2)[:, :, a, :]
                    nc.gpsimd.tensor_scalar(dst, c_in[i][:], parity[:, a:a + 1], None, ALU.mult).then_inc(c_wide_ready, 1)

            def scale_gates(g):
                pool.wait_ge(inv_ready, g + 1)
                dst = gate0[g // 2][:, :, (g % 2) * 512:(g % 2) * 512 + 512].rearrange("p b (h d) -> p b h d", d=HD)
                by = inv_den[:, :, 8 * g:8 * g + 8].unsqueeze(3).to_broadcast([P, NB, 8, HD])
                nc.gpsimd.tensor_tensor(dst, dst, by, ALU.mult).then_inc(gate_scaled, 1)

            pool.wait_ge(late_in, 16 * 4)
            pool.wait_ge(cum_ready, 1)
            pool.dma_start(t["cum_forget"], cum_t[:]).then_inc(cum_stored, 16)
            pool.wait_ge(cum_stored, 16)
            pool.dma_start(forget_bias, t["cum_forget"].partition_broadcast(P)).then_inc(cum_spread, 16)
            pool.wait_ge(cum_spread, 16)
            for part in range(4):
                hs = slice(4 * part, 4 * part + 4)
                near = neg_bias[:, 0, P:S].unsqueeze(1).to_broadcast([P, 4, P])
                nc.gpsimd.tensor_tensor(forget_bias0[:, hs, :], forget_bias[:, hs, 0:P], near, ALU.add)
                then(nc.gpsimd.tensor_tensor(forget_bias[:, hs, P:S], forget_bias[:, hs, P:S], near, ALU.add))
                far = neg_bias[:, 0, 0:P].unsqueeze(1).to_broadcast([P, 4, P])
                nc.gpsimd.tensor_tensor(forget_bias[:, hs, 0:P], forget_bias[:, hs, 0:P], far, ALU.add).then_inc(forget_bias_ready, 1)

            def waves(i):
                w = slice(2 * i, 2 * i + 2)
                TS, TT = nc.gpsimd.tensor_scalar, nc.gpsimd.tensor_tensor
                ang, r = cos_t[:, w, :], sin_t[:, w, :]
                for s in (2 * i, 2 * i + 1):
                    TS(wave_part[:, s % 2, :], steps[:], sp["lo"][:, s:s + 1], None, ALU.mult)
                    ins = TS(cos_t[:, s, :], steps[:], sp["hi"][:, s:s + 1], None, ALU.mult)
                then(ins)
                then(TS(wave_k, ang, INV_2PI, ROUND_INT, ALU.mult, ALU.add))
                then(TS(wave_k, wave_k, -ROUND_INT, None, ALU.add))
                then(TS(r, wave_k, -TWO_PI_1, None, ALU.mult))
                then(TT(ang, ang, r, ALU.add))
                then(TS(r, wave_k, -TWO_PI_2, None, ALU.mult))
                then(TT(ang, ang, r, ALU.add))
                then(TS(r, wave_k, -TWO_PI_3, None, ALU.mult))
                then(TT(ang, ang, r, ALU.add))
                then(TT(r, ang, wave_part, ALU.add))
                TS(r, r, PI, -PI, ALU.min, ALU.max).then_inc(wave_ready, 1)

            scale_gates(0)
            scale_gates(1)
            pool.wait_ge(scored, FOX_H)
            for i in range(3):
                waves(i)
            scale_gates(2)
            scale_gates(3)
            root(1, D)
            for i in range(3, 8):
                waves(i)
            for h in range(RET_H):
                pool.wait_ge(ret_var, h + 1)
                then(nc.gpsimd.tensor_scalar(ret_rstd[:, h, :], mean_var[:, h, :, 1], EPS, None, ALU.add))
                nc.gpsimd.tensor_tensor(ret_rstd[:, h, :], ret_rstd[:, h, :], neg_half[:, 0:2], ALU.pow).then_inc(ret_scale, 1)
            root(2, D)
            pool.wait_ge(h_ready, 2)
            pool.dma_start(row_a[:], t["g_post_mix_2"].partition_broadcast(P)).then_inc(row_a_in, 16)
            root(3, D)
            pool.wait_ge(rstd_ready, 4)
            then(nc.gpsimd.tensor_tensor(rstd_in[:], rstd[:, 4:6], rstd[:, 6:8], ALU.mult))
            nc.gpsimd.tensor_scalar(rstd_in_q[:], rstd_in[:], -(HD**-0.5), None, ALU.mult).then_inc(rstd_in_ready, 1)

            def rotate_out(s):
                pool.wait_ge(scan_done, s + 1)
                a = ssm_a[:, s % SSM_BUFS, :].rearrange("p (c t) -> p c t", c=2)
                b = ssm_b[:, s % SSM_BUFS, :].rearrange("p (c t) -> p c t", c=2)
                then(nc.gpsimd.tensor_tensor(a, b, cos_t[:, s, :].unsqueeze(1).to_broadcast([P, 2, S]), ALU.mult))
                then(nc.gpsimd.tensor_tensor(b, b, sin_t[:, s, :].unsqueeze(1).to_broadcast([P, 2, S]), ALU.mult))
                nc.gpsimd.tensor_tensor(a[:, 0, :], a[:, 0, :], b[:, 1, :], ALU.subtract).then_inc(prod_ready, 1)

            for s in range(ST):
                rotate_out(s)
            root(4, 512)
            root(5, 512)
            chunk_drained(pool, ("glu", 0))
            chunk_drained(pool, ("glu", 1))
            pool.dma_start(row_b[:], t["g_post_ffn_2"].partition_broadcast(P)).then_inc(row_b_in, 16)
            root(6, D)
            root(7, D)
            for c in range(11):
                pool.wait_ge(silu_ready, c + 1)
                chunk_drained(pool, ("ffn", c))
                if c >= 2:
                    pool.wait_ge(ff_lo_ready, c - 1)
                nc.gpsimd.tensor_tensor(ff_val[:, c % 2, :], ff_raw[:, c % 2, 0, :], ff_raw[:, c % 2, 1, :], ALU.mult).then_inc(ff_ready, 1)
            pool.wait_ge(row_b_in, 32)
            pool.wait_ge(squared, squared_count(7) + NB)
            nc.gpsimd.tensor_tensor(down_out[:, :, 0:512], down_out[:, :, 0:512], row_b[:, 0:512].unsqueeze(1).to_broadcast([P, NB, 512]), ALU.mult).then_inc(down_scaled, 1)
            root(8, D)

        @block.scalar
        def _(act):
            next_unit = [0]

            def split_hi(until):
                for u in range(next_unit[0], min(until, n_units)):
                    act.wait_ge(landed[u % RING], 16 * (u // RING + 1))
                    if u >= RING:
                        act.wait_ge(unit_used, u - RING + 1)
                    nc.scalar.activation(w_hi[:, u % RING, :], stage[:, u % RING, :], ACT.Copy).then_inc(hi_ready, 1)
                next_unit[0] = max(next_unit[0], min(until, n_units))

            def ahead(name):
                split_hi(last_unit[name] + 1 + AHEAD)

            n_step = [0]

            def then(ins):
                n_step[0] += 1
                ins.then_inc(act_step, 1)
                act.wait_ge(act_step, n_step[0])

            def squares(i, src, junk, sums=sumsq):
                for b in range(NB):
                    nc.scalar.activation(junk(b), src(b), ACT.Square, accum_out=sums[:, 2 * i + b:2 * i + b + 1]).then_inc(squared, 1)

            def squares_half(i, c, src):
                half = slice(c * 512, (c + 1) * 512)
                squares(i, lambda b: src[:, b, half], lambda b: junk[:, b, half], (sumsq, sumsq_b)[c])

            def hi_of_turned(first, tiles, at, gain):
                for k in range(tiles):
                    act.wait_ge(turned, first + (k | 1) + 1)
                    nc.scalar.activation(act_t[:, at + k, :], ps[:, 4 * BANK + ((at + k) % 8) * S:4 * BANK + ((at + k) % 8 + 1) * S], ACT.Copy,
                                         scale=col[:, gain + k:gain + k + 1]).then_inc(act_hi, 1)

            def out_and_turn(kind, i, first, gain):
                ahead((kind, 0))
                split_hi(chunks[(kind, 1)][0] + 4)
                chunk_drained(act, (kind, 0))
                squares_half(i, 0, x)
                split_hi(chunks[(kind, 1)][0] + 6 + AHEAD)
                hi_of_turned(first, 4, 0, gain)
                ahead((kind, 1))
                chunk_drained(act, (kind, 1))
                squares_half(i, 1, x)
                hi_of_turned(first + 4, 4, 4, gain + 4)

            def hi_of_wide(first, banks):
                for i in range(8):
                    act.wait_ge(turned, first + i + 1)
                    nc.scalar.activation(act_t[:, 2 * i:2 * i + 2, :], bank(banks[i]).rearrange("p (k n) -> p k n", k=2), ACT.Copy).then_inc(act_hi, 1)

            act.wait_ge(col_ready, 1)
            split_hi(1)
            hi_of_turned(0, KD, 0, COL_EVEN)
            split_hi(2)
            act.wait_ge(x_in, 16 * NB)
            squares(0, lambda b: x[:, b, :], lambda b: junk[:, b, :])
            split_hi(6)
            act.wait_ge(ldt_ready, 1)
            nc.scalar.activation(sp["dt"][:], sp["ldt"][:], ACT.Exp).then_inc(dt_ready, 1)
            act.wait_ge(mdt_ready, 1)
            nc.scalar.activation(sp["mag"][:], sp["mdt"][:], ACT.Exp).then_inc(mag_ready, 1)
            act.wait_ge(ang_ready, 1)
            nc.scalar.activation(sm["sin"][:], sm["r"][:], ACT.Sin)
            nc.scalar.activation(sm["cos"][:], sm["abs"][:], ACT.Sin, bias=half_pi[:], scale=-1.0).then_inc(trig_ready, 1)
            act.wait_ge(params_in, 16 * 8)
            act.wait_ge(fills, 1)
            nc.scalar.activation(wf_hi[:], wf[:], ACT.Copy).then_inc(wf_hi_ready, 1)
            for half, kind in enumerate(("ga", "gb")):
                for c in range(2):
                    ahead((kind, c))
                    chunk_done(act, (kind, c))
                    act.wait_ge(rstd_ready, 1)
                    for b in range(NB):
                        ins = nc.scalar.activation(gate0[half][:, b, c * 512:(c + 1) * 512], result((kind, c))[:, b, :], ACT.Silu, scale=rstd[:, b:b + 1])
                    ins.then_inc(drain_sem((kind, c)), 1)
            act.wait_ge(f_abs, 1)
            nc.scalar.activation(gate_f[:, 2], gate_f[:, 1], ACT.Exp).then_inc(f_exp, 1)
            act.wait_ge(f_exp, 1)
            nc.scalar.activation(gate_f[:, 3], gate_f[:, 2], ACT.Ln, bias=1.0).then_inc(f_ln, 1)

            def exponentials(n):
                act.wait_ge(scored, n + 1)
                e = prob[:, n % 3, :]
                nc.scalar.activation(e[:, 0:256], e[:, 0:256], ACT.Exp, bias=neg_max[:, 1, n:n + 1], scale=-1.0, accum_out=den[:, 1, n:n + 1])
                nc.scalar.activation(e[:, 256:384], e[:, 256:384], ACT.Exp, bias=neg_max[:, 0, n:n + 1], scale=-1.0,
                                     accum_out=den[:, 0, n:n + 1]).then_inc(exped, 1)

            for half in range(2):
                v = "va" if half == 0 else "vb"
                for c in range(2):
                    ahead((v, c))
                    if c == 1:
                        exponentials(16 * half)
                    chunk_done(act, (v, c))
                    for b in range(NB - c):
                        ins = nc.scalar.activation(v0[:, b, c * 512:(c + 1) * 512], result((v, c))[:, b, :], ACT.Copy, scale=rstd[:, b:b + 1])
                    ins.then_inc(drain_sem((v, c)), 1)
                for n in range(16 * half + 1, 16 * half + 16):
                    exponentials(n)
            hi_of_wide(KD, EVEN_TURN_BANKS)
            out_and_turn("even_out", 1, KD + 8, COL_ODD)
            for kind, n in (("rq", 2), ("rk", 2)):
                for c in range(n):
                    ahead((kind, c))
            for c in range(4):
                ahead(("rv", c))
                chunk_done(act, ("rv", c))
                for b in range(NB):
                    ins = nc.scalar.activation(v1[:, b, c * 512:(c + 1) * 512], result(("rv", c))[:, b, :], ACT.Copy, scale=rstd[:, 2 + b:3 + b])
                ins.then_inc(drain_sem(("rv", c)), 1)
            for c in range(4):
                ahead(("rg", c))
                chunk_done(act, ("rg", c))
                for b in range(NB):
                    ins = nc.scalar.activation(gate1[:, b, c * 512:(c + 1) * 512], result(("rg", c))[:, b, :], ACT.Silu, scale=rstd[:, 2 + b:3 + b])
                ins.then_inc(drain_sem(("rg", c)), 1)
                act.wait_ge(wave_ready, 2 * c + 2)
                w = slice(4 * c, 4 * c + 4)
                then(nc.scalar.activation(cos_t[:, w, :], sin_t[:, w, :], ACT.Abs))
                nc.scalar.activation(sin_t[:, w, :], sin_t[:, w, :], ACT.Sin)
                nc.scalar.activation(cos_t[:, w, :], cos_t[:, w, :], ACT.Sin, bias=half_pi[:], scale=-1.0).then_inc(wave_sin, 1)
            for h in range(RET_H):
                act.wait_ge(ret_scale, h + 1)
                act.wait_ge(ret_gated, h + 1)
                for b in range(NB):
                    o = gate1[:, b, h * RET_V:(h + 1) * RET_V]
                    ins = nc.scalar.activation(o, o, ACT.Copy, scale=ret_rstd[:, h, b:b + 1])
                ins.then_inc(ret_out, 1)
            hi_of_wide(2 * KD + 8, ODD_TURN_BANKS)
            out_and_turn("odd_out", 2, 2 * KD + 16, COL_MIX)
            split_hi(chunks[("u", 0)][0] + 5)
            act.wait_ge(h_ready, 2)
            squares(3, lambda b: x[:, b, :], lambda b: junk[:, b, :])
            ahead(("u", 0))
            split_hi(last_unit[("sq", 0)] + 1)
            act.wait_ge(rstd_in_ready, 1)
            split_hi(last_unit[("skv", 0)] + 1)
            chunk_done(act, ("sq", 0))
            for b in range(NB):
                ins = nc.scalar.activation(qkv[:, b, 0:SINK_H, :], result(("sq", 0))[:, b, :].rearrange("p (h d) -> p h d", d=HD), ACT.Copy,
                                           scale=rstd_in_q[:, b:b + 1])
            ins.then_inc(drain_sem(("sq", 0)), 1)
            chunk_done(act, ("skv", 0))
            for b in range(NB):
                ins = nc.scalar.activation(qkv[:, b, SINK_H:12, :], result(("skv", 0), 256)[:, b, :].rearrange("p (h d) -> p h d", d=HD), ACT.Copy,
                                           scale=rstd_in[:, b:b + 1])
            ins.then_inc(drain_sem(("skv", 0)), 1)
            act.wait_ge(rope_ready, 2)
            for b in range(NB):
                nc.scalar.activation(k_twice[:, b], qkv[:, b, SINK_H:SINK_H + KV_H, :].unsqueeze(2).to_broadcast([P, KV_H, 2, HD]), ACT.Copy).then_inc(k_twice_ready, 1)
            act.wait_ge(qk_turned, 1)
            nc.scalar.activation(q_t[:].rearrange("p (a m) n -> p a (m n)", a=2), ps[:, 4 * BANK:6 * BANK].rearrange("p (a n) -> p a n", a=2), ACT.Copy)
            act.wait_ge(qk_turned, 2)
            nc.scalar.activation(k_t[:], bank(3).rearrange("p (k n) -> p k n", k=2), ACT.Copy).then_inc(qk_ready, 1)
            for n in range(32, 42):
                if n in (33, 35, 37):
                    split_hi(next_unit[0] + 1)
                if n < 40:
                    exponentials(n)
                if n >= 34:
                    act.wait_ge(prob_turned, n - 1)
                    act.wait_ge(pv_done, n - 3)
                    nc.scalar.activation(prob_t[:, n % 2, :], bank(2 + n % 2, 384), ACT.Copy).then_inc(prob_copied, 1)
            act.wait_ge(sink_sum, 1)
            nc.scalar.activation(sink_exp[:], sink_exp[:], ACT.Exp).then_inc(sink_exped, 1)
            act.wait_ge(y_attn_ready, 1)
            hi_of_turned(3 * KD + 16, 4, 0, COL_GATTN)
            squares(4, lambda b: y_attn[:, b, :], lambda b: q_t[:, 2 * b:2 * b + 2, :].rearrange("p k n -> p (k n)"))

            def take_attn_half(c):
                ahead(("mix_attn", c))
                chunk_done(act, ("mix_attn", c))
                act.wait_ge(rstd_ready, 5)
                for b in range(NB):
                    ins = nc.scalar.activation(mixed[:, b, c * 512:(c + 1) * 512], result(("mix_attn", c))[:, b, :], ACT.Copy, scale=rstd[:, 8 + b:9 + b])
                ins.then_inc(drain_sem(("mix_attn", c)), 1)

            for ct in range(CT):
                act.wait_ge(y_added, ct + 1)
                nc.scalar.activation(gelu_hi[:, ct, :], y_ssm[ct], ACT.Gelu_apprx_tanh).then_inc(gelu_hi_ready, 1)
                nc.scalar.activation(y_ssm[ct], y_ssm[ct], ACT.Gelu_apprx_tanh).then_inc(gelu_ready, 1)
            take_attn_half(0)
            ahead(("glu", 1))
            chunk_drained(act, ("glu", 1))
            nc.scalar.activation(gate_z[:], gate_z[:], ACT.Sigmoid).then_inc(sig_ready, 1)
            ahead(("glu", 0))
            hi_of_turned(3 * KD + 20, 4, 4, COL_GSSM)
            squares(5, lambda b: ssm_out[:, b, :], lambda b: gate_z[:, b, :])
            take_attn_half(1)
            for c in range(2):
                ahead(("mix_ssm", c))
                for b in range(NB):
                    act.wait_ge(mixed_ready, 2 * c + b + 1)
                    half = slice(c * 512, (c + 1) * 512)
                    nc.scalar.activation(junk[:, b, half], mixed[:, b, half], ACT.Square, accum_out=(sumsq, sumsq_b)[c][:, 12 + b:13 + b]).then_inc(squared, 1)
            hi_of_turned(3 * KD + 24, KD, 0, COL_FFN)
            act.wait_ge(x_ready, 2 * NB)
            squares(7, lambda b: x[:, b, :], lambda b: junk[:, b, :])

            def ff_hi_of(c):
                act.wait_ge(ff_ready, c + 1)
                nc.scalar.activation(ff_hi[:, 2 * c:2 * c + 2, :], ff_val[:, c % 2, :].rearrange("p (k n) -> p k n", k=2), ACT.Copy).then_inc(ff_hi_ready, 1)

            for c in range(11):
                ahead(("ffn", c))
                act.wait_ge(ff_raw_ready, c + 1)
                nc.scalar.activation(ff_raw[:, c % 2, 0, :], ff_raw[:, c % 2, 0, :], ACT.Silu).then_inc(silu_ready, 1)
                if c >= 1:
                    ff_hi_of(c - 1)
            ff_hi_of(10)
            ahead(("down", 0))
            chunk_done(act, ("down", 0))
            nc.scalar.activation(down_out[:, :, 0:512], result(("down", 0)), ACT.Copy).then_inc(down_copied, 1)
            act.wait_ge(down_copied, 1)
            squares_half_down = lambda c, b, src: nc.scalar.activation(down_junk[:, b, c * 512:(c + 1) * 512], src, ACT.Square,
                                                                       accum_out=(sumsq, sumsq_b)[c][:, 16 + b:17 + b])
            for b in range(NB):
                squares_half_down(0, b, down_out[:, b, 0:512]).then_inc(squared, 1)
            ahead(("down", 1))
            chunk_done(act, ("down", 1))
            squares_half_down(1, 0, result(("down", 1))[:, 0, :]).then_inc(squared, 1)
            act.wait_ge(down_scaled_b, 1)
            squares_half_down(1, 1, result(("down", 1))[:, 1, :]).then_inc(squared, 1)

        @block.vector
        def _(dve):
            next_unit = [0]

            def split_lo(until):
                for u in range(next_unit[0], min(until, n_units)):
                    dve.wait_ge(hi_ready, u + 1)
                    nc.vector.tensor_tensor(w_lo[:, u % RING, :], stage[:, u % RING, :], w_hi[:, u % RING, :].bitcast(F32), ALU.subtract).then_inc(lo_ready, 1)
                next_unit[0] = max(next_unit[0], min(until, n_units))

            def ahead(name):
                split_lo(last_unit[name] + 1 + AHEAD)

            n_step = [0]

            def then(ins):
                n_step[0] += 1
                ins.then_inc(dve_step, 1)
                dve.wait_ge(dve_step, n_step[0])

            TT, TS, STT = nc.vector.tensor_tensor, nc.vector.tensor_scalar, nc.vector.scalar_tensor_tensor

            def spread(factors):
                for b in range(NB):
                    ins = TS(diag[:, b, :], ident[:], factors[:, b:b + 1], None, ALU.mult)
                ins.then_inc(diag_ready, 1)

            def take_row(r):
                dve.wait_ge(row_done, r + 1)
                ins = nc.vector.tensor_copy(rstd_row[:], bank(4, S))
                if r == 0:
                    then(ins)
                    ins = TS(rstd_row_q[:], rstd_row[:], -(HD**-0.5), None, ALU.mult)
                ins.then_inc(row_taken, 1)
                dve.wait_ge(row_taken, r + 1)

            def lo_of_turned(n_hi, tiles, at, gain, lo_at):
                for k in range(tiles):
                    dve.wait_ge(act_hi, n_hi + (k | 1) + 1)
                    src = ps[:, 4 * BANK + ((at + k) % 8) * S:4 * BANK + ((at + k) % 8 + 1) * S]
                    STT(act_t[:, lo_at + k, :], src, col[:, gain + k:gain + k + 1], act_t[:, at + k, :].bitcast(F32), ALU.mult, ALU.subtract).then_inc(act_lo, 1)

            def lo_of_wide(n_hi, banks):
                for i in range(8):
                    dve.wait_ge(act_hi, n_hi + i + 1)
                    TT(y_lo[:, 2 * i:2 * i + 2, :], bank(banks[i]).rearrange("p (k n) -> p k n", k=2), act_t[:, 2 * i:2 * i + 2, :].bitcast(F32), ALU.subtract).then_inc(act_lo, 1)

            nc.vector.memset(half_pi[:], PI / 2)
            nc.vector.memset(ones[:], 1.0)
            nc.vector.memset(wf[:, KD * FOX_H:W_F], 0.0)
            nc.vector.memset(neg_half[:], -0.5).then_inc(fills, 1)
            dve.wait_ge(col_turned, 1)
            then(nc.vector.tensor_copy(col[:], ps[:, 0:N_ROWS]))
            TT(col[:, COL_MIX:COL_MIX + KD], col[:, COL_MIX:COL_MIX + KD], col[:, COL_FINAL:COL_FINAL + KD], ALU.mult).then_inc(col_ready, 1)
            dve.wait_ge(col_ready, 1)
            split_lo(1)
            lo_of_turned(0, KD, 0, COL_EVEN, KD)
            split_lo(4)
            dve.wait_ge(rstd_ready, 1)
            spread(rstd[:, 0:2])
            dve.wait_ge(params_in, 16 * 8)
            dve.wait_ge(tables_in, 16 * 2)
            for a in range(2):
                r = slice(a * SSM_N, (a + 1) * SSM_N)
                ins = nc.vector.tensor_copy(sp["ldt"][r, :], log_dt[r, :].rearrange("p (t a) -> p t a", a=2)[:, :, a])
            ins.then_inc(ldt_ready, 1)
            TS(sp["lre"][:], col[:, COL_LRE:COL_LRE + ST], -1e-4, None, ALU.min)
            TS(neg_sink[:], sink[:], -1.0, None, ALU.mult)
            then(nc.vector.tensor_copy(pos[:], pos_i[:]))
            for b in range(NB):
                TS(sm["ang"][:, ST + b * ROPE_HALF:ST + (b + 1) * ROPE_HALF], inv_freq[:], pos[:, b:b + 1], None, ALU.mult)
            dve.wait_ge(dt_ready, 1)
            TT(sp["mdt"][:], sp["lre"][:], sp["dt"][:], ALU.mult).then_inc(mdt_ready, 1)
            then(TT(sm["ang"][:, 0:ST], col[:, COL_LIM:COL_LIM + ST], sp["dt"][:], ALU.mult))

            def reduce_angle(ang, k, r):
                then(TS(k, ang, INV_2PI, ROUND_INT, ALU.mult, ALU.add))
                then(TS(k, k, -ROUND_INT, None, ALU.add))
                then(STT(r, k, -TWO_PI_1, ang, ALU.mult, ALU.add))
                then(STT(r, k, -TWO_PI_2, r, ALU.mult, ALU.add))
                then(STT(r, k, -TWO_PI_3, r, ALU.mult, ALU.add))

            reduce_angle(sm["ang"][:], sm["k"][:], sm["r"][:])
            then(TS(sm["r"][:], sm["r"][:], PI, -PI, ALU.min, ALU.max))
            STT(sm["abs"][:], sm["r"][:], -1.0, sm["r"][:], ALU.mult, ALU.max).then_inc(ang_ready, 1)
            split_lo(6)
            then(TS(sp["hi"][:], sm["r"][:, 0:ST], ROUND_13, None, ALU.add))
            then(TS(sp["hi"][:], sp["hi"][:], -ROUND_13, None, ALU.add))
            then(TT(sp["lo"][:], sm["r"][:, 0:ST], sp["hi"][:], ALU.subtract))
            split_lo(last_unit[("ga", 0)] + 1)
            dve.wait_ge(mag_ready, 1)
            dve.wait_ge(trig_ready, 1)
            lre, lim = sp["lre"][:], col[:, COL_LIM:COL_LIM + ST]
            then(TT(sp["ar"][:], sp["mag"][:], sm["cos"][:, 0:ST], ALU.mult))
            then(TS(sp["ar"][:], sp["ar"][:], -1.0, None, ALU.add))
            then(TT(sp["ai"][:], sp["mag"][:], sm["sin"][:, 0:ST], ALU.mult))
            split_lo(7)
            then(TT(sp["den"][:], lre, lre, ALU.mult))
            then(TT(sp["t"][:], lim, lim, ALU.mult))
            then(TT(sp["den"][:], sp["den"][:], sp["t"][:], ALU.add))
            then(nc.vector.reciprocal(sp["den"][:], sp["den"][:]))
            then(TT(sp["fr"][:], sp["ar"][:], lre, ALU.mult))
            then(TT(sp["t"][:], sp["ai"][:], lim, ALU.mult))
            then(TT(sp["fr"][:], sp["fr"][:], sp["t"][:], ALU.add))
            then(TT(sp["fr"][:], sp["fr"][:], sp["den"][:], ALU.mult))
            then(TT(sp["fi"][:], sp["ai"][:], lre, ALU.mult))
            then(TT(sp["t"][:], sp["ar"][:], lim, ALU.mult))
            then(TT(sp["fi"][:], sp["fi"][:], sp["t"][:], ALU.subtract))
            then(TT(sp["fi"][:], sp["fi"][:], sp["den"][:], ALU.mult))
            ahead(("ga", 0))
            dve.wait_ge(wf_hi_ready, 1)
            TT(wf_lo[:], wf[:], wf_hi[:].bitcast(F32), ALU.subtract).then_inc(wf_lo_ready, 1)
            split_lo(8)
            fr_b = sp["fr"][:].unsqueeze(2).to_broadcast([P, ST, SSM_C])
            fi_b = sp["fi"][:].unsqueeze(2).to_broadcast([P, ST, SSM_C])
            dve.wait_ge(b_in_landed, 32)
            dve.wait_ge(b_wide_ready, 1)
            for i, (f0, f1, op) in enumerate(((fr_b, fi_b, ALU.subtract), (fi_b, fr_b, ALU.add))):
                TT(b_tmp[0][:], b_in[0][:], f0, ALU.mult)
                then(TT(b_tmp[1][:], b_in[1][:], f1, ALU.mult))
                for a in range(2):
                    r = slice(a * SSM_N, (a + 1) * SSM_N)
                    ins = TT(b_wide[i][r, :, a, :], b_tmp[0][r], b_tmp[1][r], op)
                if i == 0:
                    then(ins)
                    split_lo(9)
            ins.then_inc(b_wide_ready, 1)
            take_row(0)
            for c in range(1, 4):
                ahead((("ga", "ga", "gb", "gb")[c], c % 2))
            dve.wait_ge(f_done, 1)
            f_in, f_neg = gate_f[:, 0], gate_f[:, 1]
            then(TT(f_in, ps[0:FOX_H, 4 * BANK:4 * BANK + S], rstd_row[0:FOX_H, :], ALU.mult))
            then(TS(f_in, f_in, bf[:], None, ALU.add))
            STT(f_neg, f_in, -1.0, f_in, ALU.mult, ALU.min).then_inc(f_abs, 1)
            then(TS(f_in, f_in, 0.0, None, ALU.min))
            dve.wait_ge(f_ln, 1)
            then(TT(f_in, f_in, gate_f[:, 3], ALU.subtract))
            nc.vector.tensor_tensor_scan(cum_t[:], ones[0:FOX_H, 0:1].to_broadcast([FOX_H, S]), f_in, 0.0, ALU.mult, ALU.add).then_inc(cum_ready, 1)
            def take_heads(name, dst, c):
                row = rstd_row_q if name[0] == "q" else rstd_row
                ahead((name, c))
                chunk_done(dve, (name, c))
                for pair in range(2):
                    ins = TT(dst[:, 4 * c + 2 * pair:4 * c + 2 * pair + 2, :], result((name, c))[:, pair, :].rearrange("p (m n) -> p m n", m=2),
                             row[:].unsqueeze(1).to_broadcast([P, 2, S]), ALU.mult)
                ins.then_inc(drain_sem((name, c)), 1)

            take_heads("qa", q0, 0)
            take_heads("qa", q0, 1)
            dve.wait_ge(b_turned, 1)
            nc.vector.tensor_copy(b_re[:].rearrange("p t n -> p (t n)"), bank(6))
            nc.vector.tensor_copy(b_im[:].rearrange("p t n -> p (t n)"), bank(7)).then_inc(b_ready, 1)
            dve.wait_ge(c_turned, 1)
            nc.vector.tensor_copy(c_re[:].rearrange("p t n -> p (t n)"), bank(4))
            TS(c_im_neg[:].rearrange("p t n -> p (t n)"), bank(5), -1.0, None, ALU.mult).then_inc(c_ready, 1)

            def score_max(n, table):
                dve.wait_ge(scores, n + 1)
                src, dst = bank(n % 2), prob[:, n % 3, :]
                big = 3e38
                ttr = nc.vector.tensor_tensor_reduce
                if table == 0:
                    dve.wait_ge(forget_bias_ready, n // 4 + 1)
                    bias1, bias0 = forget_bias[:, n, :], forget_bias0[:, n, :]
                else:
                    bias1, bias0 = neg_bias[:, table, :], neg_bias[:, table, P:S]
                ttr(dst[:, 0:256], src[:, 0:256], bias1, 1.0, big, ALU.add, ALU.min, neg_max[:, 1, n:n + 1])
                ins = ttr(dst[:, 256:384], src[:, 256:384], bias0, 1.0, big, ALU.add, ALU.min, neg_max[:, 0, n:n + 1])
                if table == 2:
                    h = n - 32
                    then(ins)
                    m = neg_max[:, :, n:n + 1]
                    ins = TT(m, m, neg_sink[:, h:h + 1].unsqueeze(1).to_broadcast([P, NB, 1]), ALU.min)
                ins.then_inc(scored, 1)

            def copy_prob(n):
                dve.wait_ge(prob_turned, n + 1)
                if n >= 2:
                    dve.wait_ge(pv_done, n - 1)
                nc.vector.tensor_copy(prob_t[:, n % 2, :], bank(2 + n % 2, 384)).then_inc(prob_copied, 1)

            def invert(g):
                dve.wait_ge(exped, 8 * g + 8)
                nc.vector.reciprocal(inv_den[:, :, 8 * g:8 * g + 8], den[:, :, 8 * g:8 * g + 8]).then_inc(inv_ready, 1)

            def gate_heads(g):
                dve.wait_ge(pv_done, 8 * g + 8)
                dve.wait_ge(gate_scaled, g + 1)
                o = ps[:, (4 + 2 * (g % 2)) * BANK:(6 + 2 * (g % 2)) * BANK].rearrange("p (b n) -> p b n", b=2)
                dst = gate0[g // 2][:, :, (g % 2) * 512:(g % 2) * 512 + 512]
                TT(dst, o, dst, ALU.mult).then_inc(heads_out, 1)

            for half in range(2):
                if half == 1:
                    for c in range(2):
                        take_heads("qb", q0, c)
                for c in range(2):
                    take_heads(("ka", "kb")[half], k0, c)
                for c in range(2):
                    ahead((("va", "vb")[half], c))
                for i in range(16 + 4):
                    n = 16 * half + i
                    if i < 16:
                        score_max(n, half)
                    if i == 0:
                        v = (("va", "vb")[half], 1)
                        chunk_done(dve, v)
                        TS(v0[:, 1, 512:1024], result(v)[:, 1, :], rstd[:, 1:2], None, ALU.mult).then_inc(v_block_ready, 1)
                    if 2 <= i < 18:
                        copy_prob(n - 2)
                    if i % 8 == 1 and i >= 9:
                        invert((n - 9) // 8)
                    if i % 8 == 3 and i >= 11:
                        gate_heads((n - 11) // 8)

            def out_and_turn(kind, n_hi, gain):
                for c in range(2):
                    if c == 0:
                        ahead((kind, 0))
                    else:
                        split_lo(chunks[(kind, 1)][0] + 6 + AHEAD)
                        dve.wait_ge(unit_used, chunks[(kind, 1)][0] + 6)
                        lo_of_turned(n_hi, 4, 0, gain, KD)
                        ahead((kind, 1))
                    chunk_done(dve, (kind, c))
                    dst = x[:, :, c * 512:(c + 1) * 512]
                    TT(dst, result((kind, c)), dst, ALU.add).then_inc(drain_sem((kind, c)), 1)

            lo_of_wide(KD, EVEN_TURN_BANKS)
            out_and_turn("even_out", KD + 8, COL_ODD)
            lo_of_turned(KD + 12, 4, 4, COL_ODD + 4, KD + 4)
            dve.wait_ge(rstd_ready, 2)
            spread(rstd[:, 2:4])
            split_lo(last_unit[("rq", 0)] + 1)
            take_row(1)
            then(TT(rot[:], rot[:], rstd_row[:].unsqueeze(1).to_broadcast([P, 2, S]), ALU.mult))

            for kind, dst in (("rq", q1), ("rk", k1)):
                for c in range(2):
                    ahead((kind, c))
                    chunk_done(dve, (kind, c))
                    for hh in range(2):
                        h = 2 * c + hh
                        src = result((kind, c))[:, hh, :].rearrange("p (e n) -> p e n", e=2)
                        by_cos = prob_t[:, :, :].rearrange("p a b -> p (a b)")[:, 0:512].rearrange("p (e n) -> p e n", e=2)
                        by_sin = prob[:, :, :].rearrange("p a b -> p (a b)")[:, 512:1024].rearrange("p (e n) -> p e n", e=2)
                        TT(by_cos, src, rot[:, 0, :].unsqueeze(1).to_broadcast([P, 2, S]), ALU.mult)
                        ins = TT(by_sin, src, rot[:, 1, :].unsqueeze(1).to_broadcast([P, 2, S]), ALU.mult)
                        then(ins)
                        TT(dst[:, h, 0, :], by_cos[:, 0, :], by_sin[:, 1, :], ALU.subtract)
                        ins = TT(dst[:, h, 1, :], by_sin[:, 0, :], by_cos[:, 1, :], ALU.add)
                        if hh == 0:
                            then(ins)
                    ins.then_inc(drain_sem((kind, c)), 1)
                    dve.wait_ge(drain_sem((kind, c)), number[(kind, c)] // 2 + 1)
            for c in range(4):
                ahead(("rv", c))
            for c in range(4):
                ahead(("rg", c))
            for h in range(RET_H + 1):
                if h < RET_H:
                    dve.wait_ge(ret_scores, h + 1)
                    if h >= 2:
                        dve.wait_ge(ret_pv, h - 1)
                    s, d = bank(h % 2), prob_t[:, h % 2, :]
                    TT(d[:, 0:256], s[:, 0:256], decay[:, h, :], ALU.mult)
                    TT(d[:, 256:384], s[:, 256:384], decay[:, h, 0:P], ALU.mult).then_inc(ret_decayed, 1)
                if h >= 1:
                    g = h - 1
                    dve.wait_ge(ret_pv, g + 1)
                    for b in range(NB):
                        o = bank((2 if g % 2 == 0 else 4) + b)
                        then(nc.vector.bn_stats(stats[:, b, :], o))
                        ins = nc.vector.bn_aggr(mean_var[:, g, b, :], stats[:, b, :])
                        if b == 0:
                            then(ins)
                    ins.then_inc(ret_var, 1)
                    dve.wait_ge(ret_var, g + 1)
                    for b in range(NB):
                        o = bank((2 if g % 2 == 0 else 4) + b)
                        dst = gate1[:, b, g * RET_V:(g + 1) * RET_V]
                        ins = STT(dst, o, mean_var[:, g, b, 0:1], dst, ALU.subtract, ALU.mult)
                    ins.then_inc(ret_gated, 1)
            lo_of_wide(2 * KD + 8, ODD_TURN_BANKS)
            out_and_turn("odd_out", 2 * KD + 16, COL_MIX)
            lo_of_turned(2 * KD + 20, 4, 4, COL_MIX + 4, KD + 4)
            split_lo(chunks[("u", 0)][0] + 5)
            dve.wait_ge(rstd_ready, 3)
            dve.wait_ge(row_a_in, 16)
            for b in range(NB):
                ins = STT(x[:, b, :], x[:, b, :], rstd[:, 4 + b:5 + b], row_a[:], ALU.mult, ALU.mult)
                ins.then_inc(h_ready, 1)
            ahead(("u", 0))
            dve.wait_ge(rstd_in_ready, 1)
            spread(rstd_in)

            def ssm(s):
                if s in (7, 11, 15):
                    add_skip((s - 7) // 4)
                if s < ST:
                    dve.wait_ge(bu_done, s + 1)
                    if s >= SSM_BUFS:
                        dve.wait_ge(y_done, s - SSM_BUFS + 1)
                    if s % 4 == 0:
                        dve.wait_ge(wave_sin, s // 4 + 1)
                    src = bank(6).rearrange("p (c t) -> p c t", c=2)
                    a = ssm_a[:, s % SSM_BUFS, :].rearrange("p (c t) -> p c t", c=2)
                    b = ssm_b[:, s % SSM_BUFS, :].rearrange("p (c t) -> p c t", c=2)
                    TT(a, src, cos_t[:, s, :].unsqueeze(1).to_broadcast([P, 2, S]), ALU.mult)
                    TT(b, src, sin_t[:, s, :].unsqueeze(1).to_broadcast([P, 2, S]), ALU.mult).then_inc(bu_read, 1)
                    dve.wait_ge(bu_read, s + 1)
                    TT(a[:, 0, :], a[:, 0, :], b[:, 1, :], ALU.add)
                    TT(a[:, 1, :], a[:, 1, :], b[:, 0, :], ALU.subtract).then_inc(v_ready, 1)
                    dve.wait_ge(v_ready, s + 1)
                    for c in range(2):
                        ins = nc.vector.tensor_tensor_scan(b[:, c, :], sp["mag"][:, s:s + 1].to_broadcast([P, S]), a[:, c, :], 0.0, ALU.mult, ALU.add)
                    ins.then_inc(scan_done, 1)

            def add_skip(ct):
                dve.wait_ge(y_done, 4 * ct + 4)
                STT(y_ssm[ct], u_t[:, ct, :], col[:, COL_SKIP + ct:COL_SKIP + ct + 1], bank(7, S), ALU.mult, ALU.add).then_inc(y_added, 1)

            def rope(first, heads):
                for b in range(NB):
                    hs = slice(first, first + heads)
                    lo8, hi8 = qkv[:, b, hs, 0:ROPE_HALF], qkv[:, b, hs, ROPE_HALF:2 * ROPE_HALF]
                    tmp = [rope_tmp[:, 0, i * 64:i * 64 + heads * ROPE_HALF].rearrange("p (h d) -> p h d", d=ROPE_HALF) for i in range(4 * b, 4 * b + 4)]
                    at = ST + b * ROPE_HALF
                    cosb = sm["cos"][:, at:at + ROPE_HALF].unsqueeze(1).to_broadcast([P, heads, ROPE_HALF])
                    sinb = sm["sin"][:, at:at + ROPE_HALF].unsqueeze(1).to_broadcast([P, heads, ROPE_HALF])
                    TT(tmp[0], lo8, cosb, ALU.mult)
                    TT(tmp[1], hi8, sinb, ALU.mult)
                    TT(tmp[2], hi8, cosb, ALU.mult)
                    then(TT(tmp[3], lo8, sinb, ALU.mult))
                    TT(lo8, tmp[0], tmp[1], ALU.subtract)
                    ins = TT(hi8, tmp[2], tmp[3], ALU.add)
                    if b == 0:
                        then(ins)
                ins.then_inc(rope_ready, 1)

            split_lo(last_unit[("sq", 0)] + 2)
            take_row(2)
            chunk_done(dve, ("u", 0))
            for pair in range(2):
                ins = TT(u_t[:, 2 * pair:2 * pair + 2, :], result(("u", 0))[:, pair, :].rearrange("p (m n) -> p m n", m=2),
                         rstd_row[:].unsqueeze(1).to_broadcast([P, 2, S]), ALU.mult)
            ins.then_inc(drain_sem(("u", 0)), 1)
            for s_early in range(SSM_EARLY):
                if s_early == 2:
                    chunk_drained(dve, ("sq", 0))
                    rope(0, SINK_H)
                if s_early == 4:
                    chunk_drained(dve, ("skv", 0))
                    rope(SINK_H, KV_H)
                ssm(s_early)
                if s_early == 0:
                    split_lo(next_unit[0] + 1)
            s_next = SSM_EARLY
            for i in range(8 + 3):
                if i < 8:
                    score_max(32 + i, 2)
                if i >= 8:
                    split_lo(next_unit[0] + 1)
                for _ in range(SSM_STEPS[i]):
                    if s_next <= ST:
                        ssm(s_next)
                    s_next += 1
                if i == 8:
                    dve.wait_ge(scored, 40)
                    TT(sink_exp[:], neg_max[:, :, 32:40], sink[:].unsqueeze(1).to_broadcast([P, NB, SINK_H]), ALU.add).then_inc(sink_sum, 1)
            dve.wait_ge(sink_exped, 1)
            dve.wait_ge(exped, 40)
            then(TT(den[:, :, 32:40], den[:, :, 32:40], sink_exp[:], ALU.add))
            then(nc.vector.reciprocal(inv_den[:, :, 32:40], den[:, :, 32:40]))
            dve.wait_ge(pv_done, 40)
            for b in range(NB):
                ins = TT(y_attn[:, b, :].rearrange("p (h d) -> p h d", d=HD), bank(4 + b).rearrange("p (h d) -> p h d", d=HD),
                         inv_den[:, b, 32:40].unsqueeze(2).to_broadcast([P, SINK_H, HD]), ALU.mult)
            ins.then_inc(y_attn_ready, 1)
            while s_next <= ST:
                ssm(s_next)
                s_next += 1
            add_skip(3)
            lo_of_turned(3 * KD + 16, 4, 0, COL_GATTN, KD)
            for ct in range(CT):
                dve.wait_ge(gelu_ready, ct + 1)
                TT(gelu_lo[:, ct, :], y_ssm[ct], gelu_hi[:, ct, :].bitcast(F32), ALU.subtract).then_inc(gelu_lo_ready, 1)
            ahead(("mix_attn", 0))
            dve.wait_ge(row_b_in, 16)
            for c, dst in ((1, gate_z), (0, ssm_out)):
                ahead(("glu", c))
                chunk_done(dve, ("glu", c))
                for b in range(NB):
                    ins = TT(dst[:, b, :], result(("glu", c))[:, b, :], row_b[:, c * 512:(c + 1) * 512], ALU.add)
                ins.then_inc(drain_sem(("glu", c)), 1)
            chunk_drained(dve, ("glu", 0))
            dve.wait_ge(sig_ready, 1)
            TT(ssm_out[:], ssm_out[:], gate_z[:], ALU.mult).then_inc(ssm_out_ready, 1)
            lo_of_turned(3 * KD + 20, 4, 4, COL_GSSM, KD + 4)
            ahead(("mix_attn", 1))
            dve.wait_ge(rstd_ready, 6)
            dve.wait_ge(row_a_in, 32)
            for c in range(2):
                half = slice(c * 512, (c + 1) * 512)
                if c == 0:
                    ahead(("mix_ssm", 0))
                chunk_drained(dve, ("mix_attn", c))
                chunk_done(dve, ("mix_ssm", c))
                for b in range(NB):
                    ins = STT(mixed[:, b, half], result(("mix_ssm", c))[:, b, :], rstd[:, 10 + b:11 + b], mixed[:, b, half], ALU.mult, ALU.add)
                    ins.then_inc(mixed_ready, 1)
                for b in range(NB):
                    dve.wait_ge(squared, squared_count(5) + 2 * c + b + 1)
                    ins = TT(mixed[:, b, half], mixed[:, b, half], row_a[:, half], ALU.mult)
                ins.then_inc(drain_sem(("mix_ssm", c)), 1)
            split_lo(next_unit[0] + 1)
            dve.wait_ge(rstd_ready, 7)
            chunk_drained(dve, ("mix_ssm", 1))
            for c in range(2):
                for b in range(NB):
                    half = slice(c * 512, (c + 1) * 512)
                    STT(x[:, b, half], mixed[:, b, half], rstd[:, 12 + b:13 + b], x[:, b, half], ALU.mult, ALU.add).then_inc(x_ready, 1)
            lo_of_turned(3 * KD + 24, KD, 0, COL_FFN, KD)
            split_lo(last_unit[("ffn", 0)] + 1)
            dve.wait_ge(rstd_ready, 8)
            spread(rstd[:, 14:16])

            def ff_lo_of(c):
                dve.wait_ge(ff_hi_ready, c + 1)
                TT(ff_lo[:, 2 * c:2 * c + 2, :], ff_val[:, c % 2, :].rearrange("p (k n) -> p k n", k=2), ff_hi[:, 2 * c:2 * c + 2, :].bitcast(F32),
                   ALU.subtract).then_inc(ff_lo_ready, 1)

            for c in range(11):
                ahead(("ffn", c))
                if c == 0:
                    take_row(3)
                chunk_done(dve, ("ffn", c))
                if c >= 2:
                    dve.wait_ge(ff_ready, c - 1)
                for g in range(2):
                    ins = TT(ff_raw[:, c % 2, g, :].rearrange("p (m n) -> p m n", m=2), result(("ffn", c))[:, g, :].rearrange("p (m n) -> p m n", m=2),
                             rstd_row[:].unsqueeze(1).to_broadcast([P, 2, S]), ALU.mult)
                    if g == 0:
                        ins.then_inc(ff_raw_ready, 1)
                ins.then_inc(drain_sem(("ffn", c)), 1)
                if c >= 1:
                    ff_lo_of(c - 1)
            ff_lo_of(10)
            for c in range(2):
                ahead(("down", c))
            dve.wait_ge(row_b_in, 32)
            chunk_done(dve, ("down", 1))
            TT(down_out[:, 1, 512:1024], result(("down", 1))[:, 1, :], row_b[:, 512:1024], ALU.mult).then_inc(down_scaled_b, 1)
            dve.wait_ge(squared, squared_count(7) + 3)
            TT(down_out[:, 0, 512:1024], result(("down", 1))[:, 0, :], row_b[:, 512:1024], ALU.mult).then_inc(down_scaled_b, 1)
            dve.wait_ge(down_scaled_b, 2)
            dve.wait_ge(down_scaled, 1)
            dve.wait_ge(rstd_ready, 9)
            for b in range(NB):
                for c in range(2):
                    half = slice(c * 512, (c + 1) * 512)
                    STT(x[:, b, half], down_out[:, b, half], rstd[:, 16 + b:17 + b], x[:, b, half], ALU.mult, ALU.add).then_inc(h_ready, 1)

        @block.tensor
        def _(pe):
            mm = nc.tensor.matmul

            def turn_rows(src, kts, at, first_kt=0):
                for k in range(kts):
                    for b in range(NB):
                        o = 4 * BANK + ((at + k) % 8) * S + b * P
                        ins = nc.tensor.transpose(ps[:, o:o + P], src(b, first_kt + k), ident[:])
                    ins.then_inc(turned, 1)

            def row_of_diag():
                row_done_count[0] += 1
                pe.wait_ge(diag_ready, row_done_count[0])
                for b in range(NB):
                    ins = mm(bank(4, P, b * P), ones[:], diag[:, b, :], start=True, stop=True)
                ins.then_inc(row_done, 1)

            row_done_count = [0]
            turn_x = lambda first: turn_rows(lambda b, k: x[:, b, k * P:(k + 1) * P], 4, first, first)

            def turn_wide(src, lo_before, ready, banks, read_out):
                for i in range(8):
                    pe.wait_ge(ready, i // 2 + 1)
                    if i == 2:
                        pe.wait_ge(read_out, 3)
                    if i == 4:
                        pe.wait_ge(read_out, 4)
                    if i >= 6:
                        pe.wait_ge(act_lo, lo_before + i - 5)
                    for kk in range(2):
                        for b in range(NB):
                            o = banks[i] * BANK + kk * S + b * P
                            ins = nc.tensor.transpose(ps[:, o:o + P], src(b, 2 * i + kk), ident[:])
                    ins.then_inc(turned, 1)

            def start_chunk(name):
                n = number[name]
                if n >= 2:
                    pe.wait_ge(drained[n % 2], n // 2)

            def unit_of(name, j):
                u = chunks[name][0] + j
                pe.wait_ge(lo_ready, u + 1)
                per = chunks[name][2]
                view = lambda w: w[:, u % RING, :].rearrange("p (t n) -> p t n", t=per)
                return view(w_hi), view(w_lo)

            def tokens_unit(name, j, a_hi, a_lo, k_tiles, before=None):
                per = chunks[name][2]
                width = UNIT // per
                hi, lo = unit_of(name, j)
                out = result(name, width)
                for i in range(per):
                    k = j * per + i
                    if before is not None:
                        before(k)
                    for b in range(NB):
                        tok = slice(b * P, (b + 1) * P)
                        passes = ((a_hi(k)[:, tok], hi[:, i, :]), (a_hi(k)[:, tok], lo[:, i, :]), (a_lo(k)[:, tok], hi[:, i, :]))
                        for n, (left, right) in enumerate(passes):
                            ins = mm(out[:, b, :], left, right, start=(k == 0 and n == 0), stop=(k == k_tiles - 1 and n == 2))
                ins.then_inc(unit_used, 1)

            def channels_unit(name, j, k_tiles, columns, before=None):
                hi, lo = unit_of(name, j)
                out = result(name)
                for i in range(2):
                    k = 2 * j + i
                    if before is not None:
                        before(k)
                    for m in range(4):
                        o = out[:, m // 2, (m % 2) * S:(m % 2 + 1) * S]
                        passes = ((columns(hi[:, i, :], m), act_t[:, k, :]), (columns(lo[:, i, :], m), act_t[:, k, :]),
                                  (columns(hi[:, i, :], m), act_t[:, KD + k, :]))
                        for n, (left, right) in enumerate(passes):
                            ins = mm(o, left, right, start=(k == 0 and n == 0 and m % 2 == 0), stop=(k == k_tiles - 1 and n == 2), skip_group_check=True)
                ins.then_inc(unit_used, 1)

            def ffn_unit(name, j, before=None):
                hi, lo = unit_of(name, j)
                for i in range(4):
                    k = (j // 2) * 4 + i
                    if before is not None:
                        before(k)
                    for m in range(2):
                        o, w = result(name)[:, j % 2, m * S:(m + 1) * S], slice(m * P, (m + 1) * P)
                        passes = ((hi[:, i, w], act_t[:, k, :]), (lo[:, i, w], act_t[:, k, :]), (hi[:, i, w], act_t[:, KD + k, :]))
                        for n, (left, right) in enumerate(passes):
                            ins = mm(o, left, right, start=(k == 0 and n == 0 and m == 0), stop=(k == KD - 1 and n == 2), skip_group_check=True)
                ins.then_inc(unit_used, 1)

            x_hi = lambda k: act_t[:, k, :]
            x_lo = lambda k: act_t[:, KD + k, :]
            plain = lambda w, m: w[:, m * P:(m + 1) * P]

            def tokens(name, before=None):
                start_chunk(name)
                for j in range(chunks[name][1]):
                    tokens_unit(name, j, x_hi, x_lo, KD, before)

            def channels(name, columns=plain, before=None):
                start_chunk(name)
                for j in range(chunks[name][1]):
                    channels_unit(name, j, KD, columns, before)

            def after_lo(count):
                return lambda k: pe.wait_ge(act_lo, count + k + 1)

            pe.wait_ge(ident_in, 16)
            pe.wait_ge(rows_in, 16)
            nc.tensor.transpose(ps[:, 0:N_ROWS], rows[0:N_ROWS, :], ident[0:N_ROWS, 0:N_ROWS]).then_inc(col_turned, 1)
            pe.wait_ge(x_in, 16 * NB)
            turn_x(0)
            turn_x(4)
            pe.wait_ge(col_ready, 1)
            tokens(("ga", 0), after_lo(0))
            row_of_diag()
            for name in (("ga", 1), ("gb", 0), ("gb", 1)):
                tokens(name)
            pe.wait_ge(wf_lo_ready, 1)
            pe.wait_ge(row_taken, 1)
            for k in range(KD):
                w = slice(k * FOX_H, k * FOX_H + P)
                passes = ((wf_hi[:, w], x_hi(k)), (wf_lo[:, w], x_hi(k)), (wf_hi[:, w], x_lo(k)))
                for n, (left, right) in enumerate(passes):
                    ins = mm(bank(4, S), left, right, start=(k == 0 and n == 0), stop=(k == KD - 1 and n == 2))
            ins.then_inc(f_done, 1)
            channels(("qa", 0))
            channels(("qa", 1))
            pe.wait_ge(b_wide_ready, 2)
            for i in range(2):
                for ct in range(CT):
                    src = b_wide[i][:, 4 * ct:4 * ct + 4, :, :].rearrange("p t a h -> p (t a h)")
                    ins = nc.tensor.transpose(bank(6 + i, P, ct * P), src, ident[:])
            ins.then_inc(b_turned, 1)
            pe.wait_ge(c_wide_ready, 4)
            pe.wait_ge(f_abs, 1)
            for i in range(2):
                for ct in range(CT):
                    ins = nc.tensor.transpose(bank(4 + i, P, ct * P), c_wide[i][:, ct * P:(ct + 1) * P], ident[:])
            ins.then_inc(c_turned, 1)
            for name in (("ka", 0), ("ka", 1)):
                channels(name)

            def scores_of(n, q, k):
                if n >= 2:
                    pe.wait_ge(scored, n - 1)
                for at, width, tok in ((0, S, slice(P, S)), (2 * P, P, slice(0, P))):
                    ins = mm(bank(n % 2, width, at), q[:, tok], k[:, 0:width], start=True, stop=True)
                ins.then_inc(scores, 1)

            def attend(first, heads, q_of, k_of, v_of, scores_made=0, between=lambda i, part: None):
                for i in range(scores_made - 2, heads + 1):
                    if i + 2 < heads:
                        scores_of(first + i + 2, q_of(i + 2), k_of(i + 2))
                    between(i, 0)
                    if 0 <= i < heads:
                        n = first + i
                        pe.wait_ge(exped, n + 1)
                        if n >= 2:
                            pe.wait_ge(prob_copied, n - 1)
                        for part in range(3):
                            ins = nc.tensor.transpose(bank(2 + n % 2, P, part * P), prob[:, n % 3, part * P:(part + 1) * P], ident[:])
                        ins.then_inc(prob_turned, 1)
                    if i >= 1:
                        n = first + i - 1
                        g = n // 8
                        if n % 8 == 0 and 2 <= g < 4:
                            pe.wait_ge(heads_out, g - 1)
                        pe.wait_ge(prob_copied, n + 1)
                        e = prob_t[:, n % 2, :]
                        col_at = (n % 8) * HD
                        out = 4 + 2 * (g % 2)
                        mm(bank(out + 1, HD, col_at), e[:, 0:P], v_of(i - 1, 0), start=True, stop=False)
                        mm(bank(out + 1, HD, col_at), e[:, P:2 * P], v_of(i - 1, 1), start=False, stop=True)
                        mm(bank(out, HD, col_at), e[:, 2 * P:3 * P], v_of(i - 1, 0), start=True, stop=True).then_inc(pv_done, 1)
                    between(i, 1)

            def values_and_attention(half):
                rows_of = lambda i: slice((i % 2) * HD, (i % 2 + 1) * HD)
                q_of, k_of = lambda i: q0[rows_of(i), i // 2, :], lambda i: k0[rows_of(i), i // 2, :]
                v = ("va", "vb")[half]
                tokens((v, 0))
                start_chunk((v, 1))
                for j in range(4):
                    if j == 3:
                        for name in ((v, 0), (("qa", "qb")[half], 1), (("ka", "kb")[half], 0), (("ka", "kb")[half], 1)):
                            chunk_drained(pe, name)
                        scores_of(16 * half, q_of(0), k_of(0))
                    tokens_unit((v, 1), j, x_hi, x_lo, KD)
                scores_of(16 * half + 1, q_of(1), k_of(1))
                chunk_drained(pe, (v, 1))
                pe.wait_ge(v_block_ready, half + 1)
                attend(16 * half, 16, q_of, k_of, lambda i, b: v0[:, b, i * HD:(i + 1) * HD], 2)

            pe.wait_ge(c_ready, 1)
            pe.wait_ge(b_ready, 1)
            values_and_attention(0)
            for name in (("qb", 0), ("qb", 1), ("kb", 0), ("kb", 1)):
                channels(name)
            values_and_attention(1)

            def wide_out(kind, lo_before):
                for c in range(2):
                    name = (kind, c)
                    start_chunk(name)
                    for j in range(8):
                        if (c, j) == (1, 6):
                            chunk_drained(pe, (kind, 0))
                            turn_x(0)
                        tokens_unit(name, j, x_hi, lambda k: y_lo[:, k, :], 16, lambda k: pe.wait_ge(act_lo, lo_before + k // 2 + 1))

            pe.wait_ge(heads_out, 3)
            turn_wide(lambda b, k: gate0[k // 8][:, b, (k % 8) * P:(k % 8 + 1) * P], KD, heads_out, EVEN_TURN_BANKS, heads_out)
            wide_out("even_out", KD)
            pairs = lambda w, m: w[:, (m // 2) * RET_QK:(m // 2 + 1) * RET_QK].rearrange("p (n e) -> p e n", e=2)[:, m % 2, :]
            start_chunk(("rq", 0))
            for j in range(4):
                if j == 1:
                    chunk_drained(pe, ("even_out", 1))
                    turn_x(4)
                if j == 3:
                    row_of_diag()
                channels_unit(("rq", 0), j, KD, pairs, after_lo(KD + 8))
            for name in (("rq", 1), ("rk", 0), ("rk", 1)):
                channels(name, pairs)
            for kind in ("rv", "rg"):
                for c in range(4):
                    tokens((kind, c))
            chunk_drained(pe, ("rg", 2))
            chunk_drained(pe, ("rg", 3))
            for h in range(RET_H + 1):
                if h < RET_H:
                    if h >= 2:
                        pe.wait_ge(ret_decayed, h - 1)
                    for kb, q_from, at in ((0, 0, 0), (1, P, 2 * P)):
                        for e in range(2):
                            ins = mm(bank(h % 2, S - q_from, at), k1[:, h, e, kb * P:(kb + 1) * P], q1[:, h, e, q_from:S], start=(e == 0), stop=(e == 1))
                    ins.then_inc(ret_scores, 1)
                if h >= 1:
                    g = h - 1
                    pe.wait_ge(ret_decayed, g + 1)
                    if g >= 2:
                        pe.wait_ge(ret_gated, g - 1)
                    o = 2 if g % 2 == 0 else 4
                    e, vv = prob_t[:, g % 2, :], slice(g * RET_V, (g + 1) * RET_V)
                    mm(bank(o), e[:, 0:P], v1[:, 0, vv], start=True, stop=True)
                    mm(bank(o + 1), e[:, P:2 * P], v1[:, 0, vv], start=True, stop=False)
                    mm(bank(o + 1), e[:, 2 * P:3 * P], v1[:, 1, vv], start=False, stop=True).then_inc(ret_pv, 1)
            turn_wide(lambda b, k: gate1[:, b, k * P:(k + 1) * P], 2 * KD + 8, ret_out, ODD_TURN_BANKS, ret_gated)
            wide_out("odd_out", 2 * KD + 8)
            start_chunk(("u", 0))
            for j in range(4):
                if j == 1:
                    chunk_drained(pe, ("odd_out", 1))
                    turn_x(4)
                channels_unit(("u", 0), j, KD, plain, after_lo(2 * KD + 16))

            def ssm(s):
                if s < ST:
                    if s >= 1:
                        pe.wait_ge(bu_read, s)
                    ct, r = s // 4, slice(32 * (s % 4), 32 * (s % 4) + 32)
                    mm(bank(6, S, 0), b_re[r, ct, :], u_t[r, ct, :], start=True, stop=True)
                    mm(bank(6, S, S), b_im[r, ct, :], u_t[r, ct, :], start=True, stop=True).then_inc(bu_done, 1)
                if s >= 3:
                    y = s - 3
                    ct, m = y // 4, slice(32 * (y % 4), 32 * (y % 4) + 32)
                    if y % 4 == 0 and ct >= 1:
                        pe.wait_ge(y_added, ct)
                    pe.wait_ge(prod_ready, y + 1)
                    a, b = ssm_a[:, y % SSM_BUFS, :], ssm_b[:, y % SSM_BUFS, :]
                    o = ps[m, 7 * BANK:7 * BANK + S]
                    for n, (c, w) in enumerate(((c_re, a[:, 0:S]), (c_im_neg, b[:, 0:S]), (c_im_neg, a[:, S:2 * S]))):
                        ins = mm(o, c[:, ct, m], w, start=(n == 0), stop=(n == 2))
                    ins.then_inc(y_done, 1)

            start_chunk(("sq", 0))
            tokens_unit(("sq", 0), 0, x_hi, x_lo, KD)
            tokens_unit(("sq", 0), 1, x_hi, x_lo, KD)
            row_of_diag()
            tokens_unit(("sq", 0), 2, x_hi, x_lo, KD)
            chunk_drained(pe, ("u", 0))
            ssm(0)
            tokens_unit(("sq", 0), 3, x_hi, x_lo, KD)
            ssm(1)
            start_chunk(("skv", 0))
            for j in range(2):
                tokens_unit(("skv", 0), j, x_hi, x_lo, KD)
                ssm(2 + j)
            pe.wait_ge(row_taken, 3)
            pe.wait_ge(rope_ready, 1)
            for m in range(4):
                for b in range(NB):
                    ins = nc.tensor.transpose(ps[:, 4 * BANK + m * S + b * P:4 * BANK + m * S + (b + 1) * P],
                                              qkv[:, b, 2 * m:2 * m + 2, :].rearrange("p h d -> p (h d)"), ident[:])
            ins.then_inc(qk_turned, 1)
            ssm(4)
            pe.wait_ge(k_twice_ready, 2)
            for m in range(KV_H):
                for b in range(NB):
                    ins = nc.tensor.transpose(bank(3, P, m * S + b * P), k_twice[:, b, m].rearrange("p r d -> p (r d)"), ident[:])
            ins.then_inc(qk_turned, 1)
            ssm(5)
            chunk_drained(pe, ("skv", 0))
            pe.wait_ge(qk_ready, 1)

            def ssm_steps(i, part):
                if part < SSM_STEPS[i + 2]:
                    ssm(SSM_EARLY + sum(SSM_STEPS[:i + 2]) + part)

            rows_of = lambda i: slice((i % 2) * HD, (i % 2 + 1) * HD)
            attend(32, 8, lambda i: q_t[rows_of(i), i // 2, :], lambda i: k_t[rows_of(i), i // 4, :],
                   lambda i, b: qkv[:, b, SINK_H + KV_H + i // 4, :], 0, ssm_steps)
            pe.wait_ge(y_attn_ready, 1)
            turn_rows(lambda b, k: y_attn[:, b, k * P:(k + 1) * P], 4, 0)

            def mix_part(kind, c, at, before=None):
                start_chunk((kind, c))
                for j in range(2):
                    tokens_unit((kind, c), j, lambda k: x_hi(at + k), lambda k: x_lo(at + k), CT, before)

            mix_part("mix_attn", 0, 0, after_lo(3 * KD + 16))
            for c in (1, 0):
                name = ("glu", c)
                start_chunk(name)
                for j in range(2):
                    tokens_unit(name, j, lambda k: gelu_hi[:, k, :], lambda k: gelu_lo[:, k, :], CT,
                                lambda k: pe.wait_ge(gelu_lo_ready, k + 1))
            mix_part("mix_attn", 1, 0)
            pe.wait_ge(ssm_out_ready, 1)
            turn_rows(lambda b, k: ssm_out[:, b, k * P:(k + 1) * P], 4, 4)
            mix_part("mix_ssm", 0, 4, after_lo(3 * KD + 20))
            mix_part("mix_ssm", 1, 4)
            pe.wait_ge(x_ready, NB)
            turn_x(0)
            pe.wait_ge(x_ready, 2 * NB)
            turn_x(4)
            for c in range(11):
                start_chunk(("ffn", c))
                for j in range(4):
                    ffn_unit(("ffn", c), j, after_lo(3 * KD + 24) if c == 0 else None)
                if c == 0:
                    row_of_diag()
            for c in range(2):
                name = ("down", c)
                start_chunk(name)
                for j in range(KF // 2):
                    tokens_unit(name, j, lambda k: ff_hi[:, k, :], lambda k: ff_lo[:, k, :], KF, lambda k: pe.wait_ge(ff_lo_ready, k // 2 + 1))


_INPUTS = [
    "x", "even_norm", "even_w_in", "even_b_f", "even_w_out", "odd_norm", "odd_w_in", "odd_w_out", "final_norm",
    "positions_2", "g_pre_mix_2", "w_in_2", "ssm_lambda_re_2", "ssm_lambda_im_2", "ssm_log_dt_2", "ssm_b_re_2", "ssm_b_im_2",
    "ssm_c_re_2", "ssm_c_im_2", "ssm_d_2", "w_glu_2", "b_glu_2", "attn_sinks_2", "g_ssm_out_2", "g_attn_out_2", "w_out_2",
    "g_post_mix_2", "g_pre_ffn_2", "w_gate_up_2", "w_down_2", "g_post_ffn_2",
]
_MATRIX = {
    "x": (S, D), "even_w_in": (D, 8208), "even_w_out": (2048, D), "odd_w_in": (D, 6144), "odd_w_out": (2048, D),
    "w_in_2": (D, 1280), "w_glu_2": (512, 1024), "w_out_2": (D, D), "w_gate_up_2": (D, 2 * DFF), "w_down_2": (DFF, D),
    "ssm_b_re_2": (2048, 16), "ssm_b_im_2": (2048, 16), "ssm_c_re_2": (512, 64), "ssm_c_im_2": (512, 64),
}


_ROWS = ["even_norm", "odd_norm", "g_pre_mix_2", "g_pre_ffn_2", "g_ssm_out_2", "g_attn_out_2", "ssm_d_2", "ssm_lambda_re_2", "ssm_lambda_im_2",
         "final_norm"]


def kernel(**inputs):
    import numpy as _np
    import concourse.bacc as _bacc
    from concourse import mybir as _mybir
    from concourse.bass_utils import run_bass_kernel_spmd as _run

    nc = _bacc.Bacc("TRN2", target_bir_lowering=False, num_devices=1)
    arrays, t = {}, {}
    given = {n: _np.ascontiguousarray(inputs[n]).reshape(_MATRIX.get(n, (-1,))) for n in _INPUTS}
    given["vectors"] = _np.concatenate([given[n].reshape(-1, P) for n in _ROWS])
    given.update(constant_tables())
    for name, a in given.items():
        arrays["in_" + name] = a
        t[name] = nc.dram_tensor("in_" + name, a.shape, _mybir.dt.from_np(a.dtype), kind="ExternalInput").ap()
    t["cum_forget"] = nc.dram_tensor("cum_forget", (FOX_H, S), _mybir.dt.float32, kind="Internal").ap()
    t["out"] = nc.dram_tensor("out_0", (S, D), _mybir.dt.float32, kind="ExternalOutput").ap()
    build(nc, t)
    r = _run(nc, [arrays], core_ids=[0])
    return r.results[0]["out_0"].reshape(1, S, D)
```
